# Optimizing a Trainium2 kernel written in Bass

```python
import jax
import jax.numpy as jnp
from jax import lax
import numpy as np

D_MODEL = 1024
BATCH = 1
SEQ = 256
DEPTH = 1

CHUNK = 64
HEAD_DIM = 64
N_RWKV_HEADS = 8
N_FOX_HEADS = 8
D_RWKV = N_RWKV_HEADS * HEAD_DIM
D_FOX = N_FOX_HEADS * HEAD_DIM
D_MIX = D_RWKV + D_FOX
DECAY_LORA = 64
AAA_LORA = 64
GATE_LORA = 128
R_OFF = 0
K_OFF = D_RWKV
V_OFF = 2 * D_RWKV
WD_OFF = 3 * D_RWKV
AD_OFF = WD_OFF + DECAY_LORA
GD_OFF = AD_OFF + AAA_LORA
RWKV_COLS = GD_OFF + GATE_LORA
FOX_COLS = 4 * D_FOX + N_FOX_HEADS
D_IN = RWKV_COLS + FOX_COLS
Q_BLOCK = 128
N_EXPERTS = 32
TOP_K = 4
D_EXPERT = D_MODEL
SWIGLU_ALPHA = 1.702
SWIGLU_LIMIT = 7.0
EXPERT_BLOCK = 256
NORM_EPS = 1e-6
GN_EPS = 64e-5
N_MOD = 6

kernel_name = 'hybrid_rwkv7_fox_moe_adaln_block'

def rms_norm(x, g):
    xf = x.astype(jnp.float32)
    y = xf * lax.rsqrt(jnp.mean(xf * xf, axis=-1, keepdims=True) + NORM_EPS)
    return (y * g.astype(jnp.float32)).astype(x.dtype)

def modulate(h, shift, scale):
    return h * (1 + scale[:, None, :]) + shift[:, None, :]

def rwkv7_mix(p, mu_shift, w0, w2, a0, a2, g2, k_k, k_a, r_k, gn_w, gn_b):
    B, S, _ = p.shape
    out_dtype = p.dtype
    pf = p.astype(jnp.float32)
    p_prev = jnp.pad(pf, ((0, 0), (1, 0), (0, 0)))[:, :-1]
    pf = pf + mu_shift * (p_prev - pf)
    r = pf[..., R_OFF:K_OFF]
    k = pf[..., K_OFF:V_OFF]
    v = pf[..., V_OFF:WD_OFF]
    wd = pf[..., WD_OFF:AD_OFF]
    ad = pf[..., AD_OFF:GD_OFF]
    gd = pf[..., GD_OFF:RWKV_COLS]
    w = -jax.nn.softplus(-(w0 + jnp.tanh(wd) @ w2)) - 0.5
    decay = jnp.exp(-jnp.exp(w))
    a = jax.nn.sigmoid(a0 + ad @ a2)
    g = jax.nn.sigmoid(gd) @ g2
    hs = lambda t: t.reshape(B, S, N_RWKV_HEADS, HEAD_DIM)
    kk = hs(k * k_k)
    kk = kk / jnp.maximum(jnp.sqrt(jnp.sum(kk * kk, axis=-1, keepdims=True)), 1e-12)
    k = k * (1 + (a - 1) * k_a)
    r_h, k_h, v_h, d_h, a_h = hs(r), hs(k), hs(v), hs(decay), hs(a)

    def step(state, inp):
        r_t, k_t, v_t, d_t, kk_t, a_t = inp
        sa = jnp.einsum('bhvk,bhk->bhv', state, -kk_t)
        state = (state * d_t[:, :, None, :]
                 + sa[..., None] * (kk_t * a_t)[:, :, None, :]
                 + v_t[..., None] * k_t[:, :, None, :])
        y_t = jnp.einsum('bhvk,bhk->bhv', state, r_t)
        return state, y_t

    xs = tuple(jnp.moveaxis(t, 1, 0) for t in (r_h, k_h, v_h, d_h, kk, a_h))
    s0 = jnp.zeros((B, N_RWKV_HEADS, HEAD_DIM, HEAD_DIM), jnp.float32)
    _, y = lax.scan(step, s0, xs)
    y = jnp.moveaxis(y, 0, 1)
    mean = jnp.mean(y, axis=-1, keepdims=True)
    var = jnp.mean(jnp.square(y - mean), axis=-1, keepdims=True)
    y = ((y - mean) * lax.rsqrt(var + GN_EPS)).reshape(B, S, D_RWKV) * gn_w + gn_b
    bonus = jnp.sum(r_h * k_h * r_k, axis=-1, keepdims=True) * v_h
    y = y + bonus.reshape(B, S, D_RWKV)
    return (y * g).astype(out_dtype)

def fox_mix(p, b_f, q_norm_g, k_norm_g, o_norm_g):
    B, S, _ = p.shape
    hs = lambda t: t.reshape(B, S, N_FOX_HEADS, HEAD_DIM)
    q = rms_norm(hs(p[..., 0:D_FOX]), q_norm_g)
    k = rms_norm(hs(p[..., D_FOX:2 * D_FOX]), k_norm_g)
    v = hs(p[..., 2 * D_FOX:3 * D_FOX])
    og = p[..., 3 * D_FOX:4 * D_FOX]
    log_f = jax.nn.log_sigmoid(p[..., 4 * D_FOX:].astype(jnp.float32) + b_f.astype(jnp.float32))
    cum = jnp.transpose(jnp.cumsum(log_f, axis=1), (0, 2, 1))
    q, k, v = (jnp.transpose(t, (0, 2, 1, 3)) for t in (q, k, v))
    scale = HEAD_DIM ** -0.5
    outs = []
    for blk in range(S // Q_BLOCK):
        q0 = blk * Q_BLOCK
        kv_len = q0 + Q_BLOCK
        qb = q[:, :, q0:kv_len]
        kb = k[:, :, :kv_len]
        vb = v[:, :, :kv_len]
        s = jnp.einsum('bhqd,bhkd->bhqk', qb, kb).astype(jnp.float32) * scale
        s = s + cum[:, :, q0:kv_len, None] - cum[:, :, None, :kv_len]
        mask = (q0 + jnp.arange(Q_BLOCK))[:, None] >= jnp.arange(kv_len)[None, :]
        s = jnp.where(mask, s, -jnp.inf)
        pr = jax.nn.softmax(s, axis=-1)
        outs.append(jnp.einsum('bhqk,bhkd->bhqd', pr.astype(vb.dtype), vb))
    o = jnp.transpose(jnp.concatenate(outs, axis=2), (0, 2, 1, 3))
    o = rms_norm(o, o_norm_g).reshape(B, S, D_FOX)
    return o * jax.nn.sigmoid(og)

def moe_ffn(h, w_router, b_router, w_gate_up, b_gate_up, w_down, b_down):
    B, S, D = h.shape
    T = B * S
    ht = h.reshape(T, D)
    logits = (ht @ w_router).astype(jnp.float32) + b_router.astype(jnp.float32)
    top_val, top_idx = lax.top_k(logits, TOP_K)
    gates = jax.nn.softmax(top_val, axis=-1)
    n_slots = T * TOP_K
    flat_e = top_idx.reshape(-1)
    flat_tok = jnp.arange(n_slots, dtype=jnp.int32) // TOP_K
    flat_gate = gates.reshape(-1)
    order = jnp.argsort(flat_e)
    sorted_e = flat_e[order]
    counts = jnp.zeros((N_EXPERTS,), jnp.int32).at[flat_e].add(1)
    starts = jnp.cumsum(counts) - counts
    padded = (counts + EXPERT_BLOCK - 1) // EXPERT_BLOCK * EXPERT_BLOCK
    pad_ends = jnp.cumsum(padded)
    pad_starts = pad_ends - padded
    dest = pad_starts[sorted_e] + (jnp.arange(n_slots, dtype=jnp.int32) - starts[sorted_e])
    n_blocks = -(-n_slots // EXPERT_BLOCK) + N_EXPERTS
    cap = n_blocks * EXPERT_BLOCK
    buf_tok = jnp.full((cap,), T, jnp.int32).at[dest].set(flat_tok[order])
    buf_gate = jnp.zeros((cap,), jnp.float32).at[dest].set(flat_gate[order])
    block_starts = jnp.arange(n_blocks, dtype=jnp.int32) * EXPERT_BLOCK
    block_e = jnp.minimum(jnp.searchsorted(pad_ends, block_starts, side='right'), N_EXPERTS - 1)
    h_pad = jnp.concatenate([ht, jnp.zeros((1, D), ht.dtype)], axis=0)
    xb = h_pad[buf_tok].reshape(n_blocks, EXPERT_BLOCK, D)

    def expert_block(args):
        xblk, e = args
        gu = xblk @ w_gate_up[e] + b_gate_up[e]
        gate = jnp.minimum(gu[:, :D_EXPERT], SWIGLU_LIMIT)
        up = jnp.clip(gu[:, D_EXPERT:], -SWIGLU_LIMIT, SWIGLU_LIMIT)
        act = gate * jax.nn.sigmoid(SWIGLU_ALPHA * gate) * (up + 1)
        return act @ w_down[e] + b_down[e]

    yb = lax.map(expert_block, (xb, block_e))
    y = yb.reshape(cap, D) * buf_gate[:, None].astype(yb.dtype)
    out = jax.ops.segment_sum(y, buf_tok, num_segments=T + 1)[:T]
    return out.reshape(B, S, D)

def setup_inputs(seed: int = 0):
    key = jax.random.key(seed)
    ks = jax.random.split(key, 32)
    f32 = jnp.float32
    L = DEPTH
    nrm = lambda k, shape, s: jax.random.normal(k, shape, f32) * s
    gain = lambda k, shape: 1.0 + 0.05 * jax.random.normal(k, shape, f32)
    return {
        'x': nrm(ks[0], (BATCH, SEQ, D_MODEL), 1.0),
        'c': nrm(ks[1], (BATCH, D_MODEL), 1.0),
        'w_ada': nrm(ks[2], (L, D_MODEL, N_MOD * D_MODEL), D_MODEL ** -0.5),
        'b_ada': nrm(ks[3], (L, N_MOD * D_MODEL), 0.02),
        'norm1_g': gain(ks[4], (L, D_MODEL)),
        'w_in': nrm(ks[5], (L, D_MODEL, D_IN), D_MODEL ** -0.5),
        'mu_shift': jax.random.uniform(ks[6], (L, RWKV_COLS), f32),
        'w0': jax.random.uniform(ks[7], (L, D_RWKV), f32, -6.0, -1.0),
        'w2': nrm(ks[8], (L, DECAY_LORA, D_RWKV), 0.5 * DECAY_LORA ** -0.5),
        'a0': nrm(ks[9], (L, D_RWKV), 0.5),
        'a2': nrm(ks[10], (L, AAA_LORA, D_RWKV), AAA_LORA ** -0.5),
        'g2': nrm(ks[11], (L, GATE_LORA, D_RWKV), GATE_LORA ** -0.5),
        'k_k': 0.85 + nrm(ks[12], (L, D_RWKV), 0.05),
        'k_a': gain(ks[13], (L, D_RWKV)),
        'r_k': nrm(ks[14], (L, N_RWKV_HEADS, HEAD_DIM), 0.1),
        'gn_w': gain(ks[15], (L, D_RWKV)),
        'gn_b': nrm(ks[16], (L, D_RWKV), 0.02),
        'b_f': jax.random.uniform(ks[17], (L, N_FOX_HEADS), f32, 1.0, 5.0),
        'q_norm_g': gain(ks[18], (L, HEAD_DIM)),
        'k_norm_g': gain(ks[19], (L, HEAD_DIM)),
        'o_norm_g': gain(ks[20], (L, HEAD_DIM)),
        'w_out': nrm(ks[21], (L, D_MIX, D_MODEL), D_MIX ** -0.5),
        'norm2_g': gain(ks[22], (L, D_MODEL)),
        'w_router': nrm(ks[23], (L, D_MODEL, N_EXPERTS), D_MODEL ** -0.5),
        'b_router': nrm(ks[24], (L, N_EXPERTS), 0.01),
        'w_gate_up': nrm(ks[25], (L, N_EXPERTS, D_MODEL, 2 * D_EXPERT), D_MODEL ** -0.5),
        'b_gate_up': nrm(ks[26], (L, N_EXPERTS, 2 * D_EXPERT), 0.02),
        'w_down': nrm(ks[27], (L, N_EXPERTS, D_EXPERT, D_MODEL), D_EXPERT ** -0.5),
        'b_down': nrm(ks[28], (L, N_EXPERTS, D_MODEL), 0.02),
        'final_g': gain(ks[29], (D_MODEL,)),
    }

def reference(x, c, w_ada, b_ada, norm1_g, w_in, mu_shift, w0, w2, a0, a2, g2, k_k, k_a,
              r_k, gn_w, gn_b, b_f, q_norm_g, k_norm_g, o_norm_g, w_out, norm2_g,
              w_router, b_router, w_gate_up, b_gate_up, w_down, b_down, final_g):
    c_act = jax.nn.silu(c)
    for l in range(DEPTH):
        mod = c_act @ w_ada[l] + b_ada[l]
        shift1, scale1, gate1, shift2, scale2, gate2 = jnp.split(mod, N_MOD, axis=-1)
        h = modulate(rms_norm(x, norm1_g[l]), shift1, scale1)
        p = h @ w_in[l]
        y_rwkv = rwkv7_mix(p[..., :RWKV_COLS], mu_shift[l], w0[l], w2[l], a0[l], a2[l], g2[l],
                           k_k[l], k_a[l], r_k[l], gn_w[l], gn_b[l])
        y_fox = fox_mix(p[..., RWKV_COLS:], b_f[l], q_norm_g[l], k_norm_g[l], o_norm_g[l])
        y = jnp.concatenate([y_rwkv, y_fox], axis=-1) @ w_out[l]
        x = x + gate1[:, None, :] * y
        h = modulate(rms_norm(x, norm2_g[l]), shift2, scale2)
        x = x + gate2[:, None, :] * moe_ffn(h, w_router[l], b_router[l], w_gate_up[l],
                                            b_gate_up[l], w_down[l], b_down[l])
    return rms_norm(x, final_g)


_drawn_inputs = setup_inputs


def setup_inputs(seed=0):
    import zlib

    import numpy as np

    out = dict(_drawn_inputs(seed))
    spreads = {}
    factors = {'gn_w': 2.972,
     'gn_b': 4.077,
     'q_norm_g': 4.365,
     'k_norm_g': 4.3,
     'b_router': 3.106,
     'b_gate_up': 6.822,
     'b_down': 8.0}
    for name, (base, spread) in spreads.items():
        noise = np.random.default_rng([zlib.crc32(name.encode()), seed]).standard_normal(out[name].shape)
        drawn = base * np.exp(spread * noise) if base else spread * noise
        out[name] = jnp.asarray(drawn.astype(out[name].dtype))
    for name, factor in factors.items():
        out[name] = (out[name] * factor).astype(out[name].dtype)
    return out
```

```python
import concourse.bass as bass
from concourse import mybir
from contextlib import ExitStack

F32 = mybir.dt.float32
F32R = mybir.dt.float32r
I32 = mybir.dt.int32
I8 = mybir.dt.int8
U32 = mybir.dt.uint32
ALU = mybir.AluOpType
ACT = mybir.ActivationFunctionType
AX = mybir.AxisListType

P = 128
D = 1024
KT = D // P
T = 256
TT = T // P
HD = 64
NH = 8
NF = NH * HD // P
NC = 512
RT = 14
INT = 31
NU = NH * TT
NE = 32
TOPK = 4
CAP = 64
NI = NE + T * TOPK // CAP
RING = 6
NADA = 6 * D // NC
NIN = 8
NOUT = D // NC
EC = 6
LEVELS = (1, 2, 4, 8, 16, 32, 64)
NORM_EPS = 1e-6
GN_EPS = 64e-5
EXPM05 = 0.6065306597126334
ALPHA = 1.702
LIMIT = 7.0

ROWS = [('c', 8), ('norm1_g', 8), ('mu_shift', 14), ('w0', 4), ('a0', 4), ('k_k', 4), ('k_a', 4),
        ('r_k', 4), ('gn_w', 4), ('gn_b', 4), ('q_norm_g', 1), ('k_norm_g', 1), ('o_norm_g', 1)]
ROW = {}
for _name, _n in ROWS:
    ROW[_name] = sum(n for m, n in ROWS[:len(ROW)])
NROW = sum(n for _, n in ROWS)


def build(nc, x, c, w_ada, b_ada, norm1_g, w_in, mu_shift, w0, w2, a0, a2, g2, k_k, k_a, r_k, gn_w,
          gn_b, b_f, q_norm_g, k_norm_g, o_norm_g, w_out, norm2_g, w_router, b_router, w_gate_up,
          b_gate_up, w_down, b_down, final_g, out, dbg=None):
    ctx = ExitStack()
    with ctx:
        sems = {}

        def S(name):
            if name not in sems:
                sems[name] = ctx.enter_context(nc.semaphore(name))
            return sems[name]

        def place(name, shape, dt, offset):
            n = 1 if dt == I8 else 4
            for d in shape[1:]:
                n *= d
            assert offset + n <= nc.sbuf_usable_end, (name, offset + n - nc.sbuf_usable_end)
            return nc.alloc_sbuf_tensor_at(name, list(shape), dt, offset=offset), offset + (n + 31) // 32 * 32

        class Region:

            def __init__(self, offset):
                self.at = offset

            def __call__(self, name, shape, dt=F32):
                t, self.at = place(name, shape, dt, self.at)
                return t

        both = Region((nc.sbuf_base + 63) // 64 * 64)
        raw = both("raw", [P, RING, KT, NC])
        ident = both("ident", [P, P])
        items = both("items", [1, NI + 2], I32)
        n_items = both("n_items", [1, 2], I32)
        pos = both("pos", [P, TT, NE])
        gates = both("gates", [P, TT, NE])
        slots = both("slots", [P, 2, CAP])
        base = both.at

        moe = Region(base)
        w_hi = moe("w_hi", [P, 2, KT, NC], F32R)
        w_lo = moe("w_lo", [P, 2, KT, NC], F32R)
        h_hi = moe("h_hi", [P, TT, D], F32R)
        h_lo = moe("h_lo", [P, TT, D], F32R)
        xT = moe("xT", [P, KT, 2, CAP], F32R)
        aT = moe("aT", [P, KT, 2, CAP], F32R)
        xg = moe("xg", [P, D])
        evac = moe("evac", [P, 3, NC])
        biasT = moe("biasT", [P, NE, 4, 4])
        bias_i = moe("bias_i", [P, 4, 4])
        onehot = moe("onehot", [P, TT, 2, CAP], F32R)
        gatehot = moe("gatehot", [P, TT, 2, CAP])
        scat = moe("scat", [P, T])
        gated = moe("gated", [P, 4, CAP])
        sig = moe("sig", [P, 4, CAP])
        ups = moe("ups", [P, 4, CAP])

        SLOT = 4096

        def at_slot(n, name, shape, dt=F32, off=0):
            return place(name, shape, dt, base + n * SLOT + off)[0]

        pz = at_slot(0, "pz", [P, RT, T + 1])
        AR = at_slot(0, "AR", [P, NF, TT, 2, P])
        Kr = at_slot(2, "Kr", [P, NF, TT, P])
        nBr = at_slot(3, "nBr", [P, NF, TT, P])
        x_sb = at_slot(4, "x_sb", [P, TT, D])
        r_f = at_slot(4, "r_f", [P, NF, T])
        k_f = at_slot(5, "k_f", [P, NF, T])
        v_f = at_slot(6, "v_f", [P, NF, T])
        logd = at_slot(7, "logd", [P, NF, T])
        a_f = at_slot(8, "a_f", [P, NF, T])
        kk_f = at_slot(9, "kk_f", [P, NF, T])
        b_f_ = at_slot(10, "b_f_", [P, NF, T])
        cum = at_slot(11, "cum", [P, NF, T])
        LR = at_slot(4, "LR", [P, NU, 4, P])
        pf = at_slot(12, "pf", [P, 16, T])
        Ti = at_slot(12, "Ti", [P, NU, P])
        TiT = at_slot(14, "TiT", [P, NU, P])
        lora = at_slot(16, "lora", [P, 2, T])
        loraa = at_slot(16, "loraa", [P, 2, T], off=2048)
        e_a = at_slot(16, "e_a", [P, NF, T])
        fvt = at_slot(16, "fvt", [P, TT, NH * HD])
        XT_ = at_slot(16, "XT_", [P, 2, 4, P])
        dtmp = at_slot(17, "dtmp", [P, NF, T])
        pr = at_slot(17, "pr", [P, 2, 3 * P])
        mix_r = at_slot(17, "mix_r", [P, NF, T])
        e_b = at_slot(18, "e_b", [P, NF, T])
        mix_f = at_slot(18, "mix_f", [P, NF, T])
        g_f = at_slot(19, "g_f", [P, NF, T])
        lora_w = at_slot(20, "lora_w", [P, NC])
        g2_sb = at_slot(20, "g2_sb", [P, NC], off=2048)
        bonus = at_slot(20, "bonus", [P, NF, T])
        acc = at_slot(21, "acc", [P, 2, NC])
        R0 = at_slot(21, "R0", [P, NF, P])
        nBbt = at_slot(21, "nBbt", [P, NC], off=2048)
        hT = at_slot(22, "hT", [P, KT, T])
        Vt = at_slot(22, "Vt", [P, TT, NC])
        A0t = at_slot(23, "A0t", [P, NC])
        Kbt = at_slot(23, "Kbt", [P, NC], off=2048)
        binit = at_slot(24, "binit", [P, NC])
        A0 = at_slot(24, "A0", [P, NF, P])
        Kb = at_slot(24, "Kb", [P, NF, P], off=2048)
        nBb = at_slot(17, "nBb", [P, NF, P], off=2048)
        fsq = at_slot(24, "fsq", [P, NF, T])
        prT = at_slot(24, "prT", [P, 2, 3 * P])
        tail = Region(base + 25 * SLOT)
        ones = tail("ones", [P, P])
        blk = tail("blk", [P, P])
        lrmask = tail("lrmask", [P, 2, P], I32)
        lev = tail("lev", [P, len(LEVELS), P], I8)
        levT = tail("levT", [P, len(LEVELS), P], I8)
        causal = tail("causal", [P, P])
        colv = tail("colv", [P, NROW])
        fz = tail("fz", [NH, T])
        ncum = tail("ncum", [NH, T])
        arow = at_slot(24, "arow", [1, NC], off=2048)
        rowv = at_slot(16, "rowv", [NROW, P])
        xsq = at_slot(8, "xsq", [P, TT, D])
        csil = tail("csil", [P, KT])
        modc = tail("modc", [P, 16])
        ss = tail("ss", [P, 2])
        rs = tail("rs", [P, 2])
        bfc = tail("bfc", [NH, 1])
        nmid = tail("nmid", [P, NF, TT])
        rmax = tail("rmax", [P, 2, 2])
        rsum = tail("rsum", [P, 2, 2])
        rinv = tail("rinv", [P, 2, 2])
        TMV = at_slot(0, "TMV", [P, TT, NC])
        TA = at_slot(1, "TA", [P, NC])
        MV = at_slot(24, "MV", [P, TT, NC])
        QT = at_slot(2, "QT", [P, NF, P])
        Z1 = at_slot(3, "Z1", [P, NF, HD])
        ysq = at_slot(22, "ysq", [P, NF, T])
        yrs = at_slot(23, "yrs", [P, NF, T])
        yT = at_slot(24, "yT", [P, NF, T])
        x1 = at_slot(4, "x1", [P, TT, D])
        gate1 = at_slot(6, "gate1", [P, D])
        shift2 = at_slot(7, "shift2", [P, D])
        scale2 = at_slot(8, "scale2", [P, D])
        n2g = at_slot(9, "n2g", [P, D])
        h2 = at_slot(10, "h2", [P, TT, D])
        h2T = at_slot(12, "h2T", [P, KT, T])
        bgu = at_slot(14, "bgu", [NE, 2 * D])
        wr = at_slot(0, "wr", [P, KT, NE])
        bdn = at_slot(1, "bdn", [NE, D])
        rt = Region(base + 2 * SLOT)
        brt = rt("brt", [P, NE])
        logits = rt("logits", [P, TT, NE])
        top8 = rt("top8", [P, TT, 8])
        idx8 = rt("idx8", [P, TT, 8], U32)
        idxf = rt("idxf", [P, TT, 8])
        texp = rt("texp", [P, TT, TOPK])
        tsum = rt("tsum", [P, TT])
        gk = rt("gk", [P, TT, TOPK, NE])
        sel = rt("sel", [P, TT, NE])
        cnt = rt("cnt", [P, NE])
        ge = rt("ge", [P, 4, NE])
        nblk = rt("nblk", [P, NE])
        binc = rt("binc", [P, NE])
        bexc = rt("bexc", [P, NE])
        gT = rt("gT", [NE, T])
        stri = rt("stri", [P, P])
        iota_e = rt("iota_e", [P, NE])
        iota_i = rt("iota_i", [1, NI + 2])
        icmp = at_slot(20, "icmp", [1, NI + 2, NE])
        isum = rt("isum", [1, NI + 2])
        ss2 = rt("ss2", [P, 2])
        rs2 = rt("rs2", [P, 2])
        assert rt.at <= base + 4 * SLOT
        x1q = at_slot(22, "x1q", [P, D])
        yo = at_slot(4, "yo", [P, TT, D])
        yq = at_slot(6, "yq", [P, D])
        ss3 = at_slot(7, "ss3", [P, 2])
        rs3 = at_slot(7, "rs3", [P, 2], off=64)

        mod_d = nc.dram_tensor("mod_rows", [4 * D], F32, kind="Internal").ap()
        x1_d = nc.dram_tensor("x1_rows", [T, D], F32, kind="Internal").ap()

        bank = [ctx.enter_context(nc.psum_tensor(f"bank{i}", [P, NC], F32)) for i in range(8)]

        def wview(w):
            return w.rearrange("(k p) n -> p k n", p=P)

        stream = [('ada', j) for j in range(4)]
        for j in range(NIN):
            stream += [('in', j), ('ada', 4 + j)]
        stream += [('out', j) for j in range(NOUT)]
        NS = len(stream)
        where = {u: n for n, u in enumerate(stream)}

        def slot_of(n):
            return n % RING

        def loaded(n):
            return S(f"w_loaded{n % RING}"), 16 * (n // RING + 1)

        def used(n):
            kind, j = stream[n]
            return {'ada': (S("ada_used"), j + 1), 'in': (S("p_mm"), min(4 * j + 4, INT)),
                    'out': (S("wo_mm"), TT * (j + 1))}[kind]

        def item_slot(cc):
            return (NS + cc) % RING

        def item_loaded(cc):
            return S(f"w_loaded{item_slot(cc)}"), 16 * ((NS + cc) // RING + 1)


        ACC = (2, 0, 1, 2, 0, 1)
        GU_COLS = [0, D, NC, D + NC]
        gu_view = w_gate_up[0].rearrange("e (k p) n -> e p k n", p=P)
        dn_view = w_down[0].rearrange("e (k p) n -> e p k n", p=P)

        def chunk_src(e, cc):
            if cc < 4:
                at0 = GU_COLS[cc]
                return gu_view[bass.ds(e, 1), :, :, at0:at0 + NC].rearrange("e p k n -> (e p) k n")
            return dn_view[bass.ds(e, 1), :, 4 * (cc - 4):4 * (cc - 3), :].rearrange("e p k n -> (e p) k n")

        def chunk_dst(cc):
            dst = raw[:, item_slot(cc), :, :]
            return dst if cc < 4 else dst.rearrange("p (k h) n -> p k (h n)", h=2)

        last = raw[:, item_slot(0), :, :].rearrange("p k n -> p (k n)")
        x1e, gate2, fg = last[:, 0:2 * D], last[:, 2 * D:3 * D], last[:, 3 * D:4 * D]

        def tile_of(h):
            return h // 2, slice(HD * (h % 2), HD * (h % 2) + HD)

        def colof(name, i=0, n=1):
            return colv[:, ROW[name] + i:ROW[name] + i + n]

        block = ctx.enter_context(nc.Block())

        @block.sync
        def _(sp):
            sp.dma_start(x_sb[:, :, :], x[0].rearrange("(t p) n -> p t n", p=P)).then_inc(S("x_in"), 16)
            for n, (kind, j) in enumerate(stream):
                if n >= RING:
                    sp.wait_ge(*used(n - RING))
                src = {'ada': w_ada, 'in': w_in, 'out': w_out}[kind][0]
                w = min(NC, src.shape[1] - j * NC)
                sp.dma_start(raw[:, n % RING, :, 0:w], wview(src)[:, :, j * NC:j * NC + w])\
                  .then_inc(S(f"w_loaded{n % RING}"), 16)
            for cc in range(EC):
                sp.wait_ge(*used(NS + cc - RING))
                sp.dma_start(chunk_dst(cc), chunk_src(0, cc))\
                  .then_inc(S(f"w_loaded{item_slot(cc)}"), 16)
            sp.wait_ge(S("items_ready"), 2)
            n_it = sp.value_load(n_items[0:1, 0:1], min_val=0, max_val=NI - NE) + NE
            with sp.Fori(1, n_it) as i:
                e = sp.value_load(items[0:1, bass.ds(i, 1)], min_val=0, max_val=NE - 1)
                for cc in range(EC):
                    sp.wait_ge(S("lo_ready"), ((i - 1) * EC + cc + 1) * 2)
                    sp.dma_start(chunk_dst(cc), chunk_src(e, cc))\
                      .then_inc(S(f"w_loaded{item_slot(cc)}"), 16)
            sp.wait_ge(S("lo_ready"), (n_it - 1) * (EC * 2) + 2)
            sp.wait_ge(S("x1_out"), 16)
            sp.dma_start(x1e.rearrange("p (t n) -> p t n", t=TT), x1_d.rearrange("(t p) n -> p t n", p=P))\
              .then_inc(S("end_in"), 16)
            sp.dma_start(gate2, mod_d[3 * D:4 * D].partition_broadcast(P)).then_inc(S("end_in"), 16)
            sp.dma_start(fg, final_g.partition_broadcast(P)).then_inc(S("end_in"), 16)
            sp.wait_ge(S("out_ready"), TT)
            sp.dma_start(out[0].rearrange("(t p) n -> p t n", p=P), yo[:, :, :]).then_inc(S("out_done"), 16)
            sp.wait_ge(S("out_done"), 16)

        @block.gpsimd
        def _(pool):
            made = [0]

            def step(ins):
                made[0] += 1
                ins.then_inc(S("pool_step"), 1)
                pool.wait_ge(S("pool_step"), made[0])

            g = nc.gpsimd

            def keep(t, pattern, base_, mult, op=ALU.is_ge, fill=0.0):
                step(g.affine_select(out=t, in_=t, compare_op=op, fill=fill, base=base_,
                                     pattern=pattern, channel_multiplier=mult))

            step(g.memset(ident[:, :], 0.0))
            keep(ident[:, :], [[-1, P]], 0, 1, ALU.not_equal, 1.0)
            step(g.memset(binit[:, :], 0.0))
            g.memset(ones[:, :], 1.0).then_inc(S("consts"), 1)
            def bias_in(j):
                if j:
                    pool.wait_ge(S("binit_used"), j)
                pool.dma_start(binit[0:1, :], b_ada[0:1, j * NC:(j + 1) * NC]).then_inc(S("binit_in"), 16)
            bias_in(0)
            bias_in(1)
            step(g.memset(blk[:, :], 1.0))
            keep(blk[:, HD:P], [[0, HD]], -HD, 1)
            keep(blk[:, 0:HD], [[0, HD]], HD - 1, -1)
            bias_in(2)
            step(g.memset(lrmask[:, :, :], 1))
            keep(lrmask[:, 0, :], [[1, P]], -1, -1)
            keep(lrmask[:, 1, :], [[1, P]], 0, -1)
            step(g.memset(causal[:, :], 0.0))
            keep(causal[:, :], [[-1, P]], 0, 1, ALU.is_ge, -1e30)
            bias_in(3)
            step(g.memset(lev[:, :, :], 0))
            step(g.memset(levT[:, :, :], 0))
            for n, m in enumerate(LEVELS):
                nb = P // (2 * m)
                for t, half, lo_, hi_ in ((lev, 0, m, 2 * m - 1), (levT, 1, 0, m - 1)):
                    v = t[:, n, :].rearrange("p (b w) -> p b w", w=2 * m)[:, :, half * m:half * m + m]
                    step(g.memset(v, 1))
                    keep(v, [[-2 * m, nb], [0, m]], -lo_, 1)
                    keep(v, [[2 * m, nb], [0, m]], hi_, -1)
            g.iota(slots[:, :, :], pattern=[[0, 2], [1, CAP]], base=0, channel_multiplier=0,
                   allow_small_or_imprecise_dtypes=True).then_inc(S("consts"), 1)
            for j in range(4, NADA):
                bias_in(j)
            pool.wait_ge(S("ew_done"), 1)
            pool.wait_ge(S("tm_T"), 2)
            g.memset(LR[:, :, :, :], 0.0).then_inc(S("LR_zero"), 1)
            pool.wait_ge(S("mixf_ready"), 1)
            for t in (Ti, TiT):
                g.tensor_copy(t[:, :, :], ident[:, :].unsqueeze(1).to_broadcast([P, NU, P]))\
                 .then_inc(S("T_ident"), 1)
            pool.wait_ge(S("y_mm"), 3)
            pool.wait_ge(S("mod_out"), 16 * 8)
            pool.dma_start(x1[:, :, :], x[0].rearrange("(t p) n -> p t n", p=P)).then_inc(S("late_in"), 16)
            for n, t in enumerate((gate1, shift2, scale2)):
                pool.dma_start(t[:, :], mod_d[n * D:(n + 1) * D].partition_broadcast(P))\
                    .then_inc(S("late_in"), 16)
            pool.dma_start(n2g[:, :], norm2_g[0].partition_broadcast(P)).then_inc(S("late_in"), 16)
            pool.dma_start(wr[:, :, :], wview(w_router[0])).then_inc(S("late2_in"), 16)
            pool.dma_start(bdn[:, :], b_down[0]).then_inc(S("late2_in"), 16)
            pool.dma_start(bgu[:, :], b_gate_up[0]).then_inc(S("late2_in"), 16)
            pool.dma_start(brt[:, :], b_router[0].partition_broadcast(P)).then_inc(S("late2_in"), 16)
            step(g.memset(stri[:, :], 1.0))
            keep(stri[:, :], [[1, P]], -1, -1)
            g.iota(iota_e[:, :], pattern=[[1, NE]], base=0, channel_multiplier=0,
                   allow_small_or_imprecise_dtypes=True).then_inc(S("late_consts"), 1)
            g.iota(iota_i[:, :], pattern=[[1, NI + 2]], base=0, channel_multiplier=0,
                   allow_small_or_imprecise_dtypes=True).then_inc(S("late_consts"), 1)
            pool.wait_ge(S("x1_ready"), 4)
            pool.dma_start(x1_d.rearrange("(t p) n -> p t n", p=P), x1[:, :, :]).then_inc(S("x1_out"), 16)
            pool.wait_ge(S("x1_out"), 16)

        @block.scalar
        def _(act_e):
            a = nc.scalar
            nrows = 0
            for name, src in (('c', c[0]), ('norm1_g', norm1_g[0]), ('mu_shift', mu_shift[0]), ('w0', w0[0]),
                              ('a0', a0[0]), ('k_k', k_k[0]), ('k_a', k_a[0]), ('gn_w', gn_w[0]),
                              ('gn_b', gn_b[0])):
                n = src.shape[0] // P
                act_e.dma_start(rowv[ROW[name]:ROW[name] + n, :], src.rearrange("(r n) -> r n", n=P))\
                     .then_inc(S("rows_in"), 16)
                nrows += 1
            act_e.dma_start(rowv[ROW['r_k']:ROW['r_k'] + 4, :], r_k[0].rearrange("(r h) n -> r (h n)", h=2))\
                 .then_inc(S("rows_in"), 16)
            nrows += 1
            for name, src in (('q_norm_g', q_norm_g), ('k_norm_g', k_norm_g), ('o_norm_g', o_norm_g)):
                for half in range(2):
                    act_e.dma_start(rowv[ROW[name]:ROW[name] + 1, HD * half:HD * half + HD], src)\
                         .then_inc(S("rows_in"), 16)
                    nrows += 1
            assert nrows == NROWDMA
            act_e.dma_start(lora_w[0:HD, :], w2[0]).then_inc(S("lora_in"), 16)
            act_e.dma_start(lora_w[HD:P, :], a2[0]).then_inc(S("lora_in"), 16)
            act_e.dma_start(g2_sb[:, :], g2[0]).then_inc(S("lora_in"), 16)
            act_e.dma_start(bfc[:, :], b_f.rearrange("o h -> h o")).then_inc(S("bf_in"), 16)

            act_e.wait_ge(S("x_in"), 16)
            for t in range(TT):
                a.activation(xsq[:, t, :], x_sb[:, t, :], ACT.Square, accum_out=ss[:, t:t + 1])\
                 .then_inc(S("ss_ready"), 1)
            act_e.wait_ge(S("ms_ready"), 1)
            a.activation(rs[:, :], ss[:, :], ACT.Sqrt).then_inc(S("rms_ready"), 1)
            act_e.wait_ge(S("colv_ready"), 1)
            a.activation(csil[:, :], colof('c', 0, 8), ACT.Sigmoid).then_inc(S("csig"), 1)
            act_e.wait_ge(S("modc_ready"), 1)
            for k in range(KT):
                act_e.wait_ge(S("xnT"), k // 2 + 1)
                a.activation(hT[:, k, :], bank[k // 2][:, (k % 2) * T:(k % 2) * T + T], ACT.Identity,
                             bias=modc[:, k:k + 1], scale=modc[:, 8 + k:9 + k]).then_inc(S("hT_ready"), 1)

            def take_tile(m):
                act_e.wait_ge(S("p_mm"), m + 1)
                if m < RT:
                    i = a.activation(pz[:, m, 1:T + 1], bank[m % 4][:, 0:T], ACT.Copy)
                elif m < INT - 1:
                    i = a.activation(pf[:, m - RT, :], bank[m % 4][:, 0:T], ACT.Copy)
                else:
                    act_e.wait_ge(S("bf_in"), 16)
                    i = a.activation(fz[:, :], bank[m % 4][0:NH, 0:T], ACT.Identity, bias=bfc[:, 0:1])
                i.then_inc(S("p_ev"), 1)

            def mod_row(j):
                act_e.wait_ge(S("acc_used"), 5 + j)
                if j:
                    act_e.wait_ge(S("mod_out"), 16 * j)
                a.activation(arow[0:1, :], bank[4][0:1, :], ACT.Copy).then_inc(S("arow_ready"), 1)
                act_e.wait_ge(S("arow_ready"), j + 1)
                act_e.dma_start(mod_d[j * NC:(j + 1) * NC].rearrange("(o n) -> o n", o=1), arow[0:1, :])\
                     .then_inc(S("mod_out"), 16)

            for m in range(16):
                take_tile(m)
                if m in (7, 11, 15):
                    mod_row((m - 7) // 4)
            act_e.wait_ge(S("shifted"), 4)
            a.activation(loraa[0:HD, 0, :], lora[0:HD, 0, :], ACT.Tanh)
            a.activation(loraa[HD:P, 0, :], lora[HD:P, 0, :], ACT.Copy)
            a.activation(loraa[:, 1, :], lora[:, 1, :], ACT.Sigmoid).then_inc(S("lora_act"), 1)
            take_tile(16)
            take_tile(17)
            for q in range(6):
                act_e.wait_ge(S("lora_mm"), q + 1)
                for t in range(2):
                    m = 2 * (q % 2) + t
                    src = bank[5 + q % 3][:, t * T:(t + 1) * T]
                    if q < 2:
                        i = a.activation(logd[:, m, :], src, ACT.Sigmoid, bias=colof('w0', m))
                    elif q < 4:
                        i = a.activation(a_f[:, m, :], src, ACT.Sigmoid, bias=colof('a0', m))
                    else:
                        i = a.activation(g_f[:, m, :], src, ACT.Copy)
                i.then_inc(S("lora_ev"), 1)
            take_tile(18)
            take_tile(19)
            mod_row(3)
            for m in (20, 21):
                take_tile(m)
            for t in range(2):
                act_e.wait_ge(S("kksum_mm"), t + 1)
                a.activation(e_b[:, 2 * t:2 * t + 2, :], bank[5 + t][:, :].rearrange("p (m t) -> p m t", m=2),
                             ACT.Sqrt).then_inc(S("kknorm"), 1)
            take_tile(22)
            take_tile(23)
            mod_row(4)
            for m in (24, 25):
                take_tile(m)
            act_e.wait_ge(S("d1_ready"), 1)
            a.activation(e_a[:, :, :], dtmp[:, :, :], ACT.Exp).then_inc(S("exps"), 1)
            a.activation(e_b[:, :, :], dtmp[:, :, :], ACT.Exp, scale=-1.0).then_inc(S("exps"), 1)
            take_tile(26)
            take_tile(27)
            mod_row(5)
            act_e.wait_ge(S("d2_ready"), 1)
            a.activation(e_a[:, :, :], dtmp[:, :, :], ACT.Exp).then_inc(S("exps"), 1)
            take_tile(28)
            take_tile(29)
            take_tile(30)
            mod_row(6)
            mod_row(7)
            act_e.wait_ge(S("d3_ready"), 1)
            a.activation(e_b[:, :, 0:P], cum[:, :, P:T], ACT.Exp).then_inc(S("exps"), 1)
            a.activation(e_a[:, :, 0:P], e_a[:, :, P:T], ACT.Exp).then_inc(S("exps"), 1)
            act_e.wait_ge(S("d4_ready"), 1)
            a.activation(e_b[:, :, P:T], dtmp[:, 0:2, :].rearrange("p m (h t) -> p (m h) t", h=2), ACT.Exp,
                         scale=-1.0).then_inc(S("exps"), 1)
            act_e.wait_ge(S("fabs"), 1)
            a.activation(ncum[:, :], ncum[:, :], ACT.Exp).then_inc(S("fexp"), 1)
            act_e.wait_ge(S("fexp"), 1)
            a.activation(ncum[:, :], ncum[:, :], ACT.Ln, bias=1.0).then_inc(S("fln"), 1)
            act_e.wait_ge(S("acc_used"), NADA)
            for n, (dst, src) in enumerate(((Vt[:, 0, :], bank[5]), (Vt[:, 1, :], bank[6]), (A0t[:, :], bank[7]),
                                            (Kbt[:, :], bank[0]), (nBbt[:, :], bank[1]))):
                act_e.wait_ge(S("tm_T"), n + 1)
                a.activation(dst, src[:, :], ACT.Copy).then_inc(S("tm_ev"), 1)
            for n in range(2):
                act_e.wait_ge(S("fms"), n + 1)
                a.activation(fsq[:, :, :], fsq[:, :, :], ACT.Sqrt).then_inc(S("frms"), 1)
            for t in range(TT):
                act_e.wait_ge(S("fv_T"), t + 1)
                a.activation(fvt[:, t, :], bank[5 + t][:, :], ACT.Copy).then_inc(S("fv_ev"), 1)
            for h in range(NH):
                act_e.wait_ge(S("smax"), h + 1)
                for t in range(TT):
                    cols = slice(0, P) if t == 0 else slice(P, 3 * P)
                    i = a.activation(pr[:, h % 2, cols], pr[:, h % 2, cols], ACT.Exp, bias=rmax[:, h % 2, t:t + 1],
                                     accum_out=rsum[:, h % 2, t:t + 1])
                i.then_inc(S("sexp"), 1)
                if h:
                    act_e.wait_ge(S("pr_T"), h)
                    if h >= 3:
                        act_e.wait_ge(S("o_mm"), h - 2)
                    a.activation(prT[:, (h - 1) % 2, :], bank[5 + (h - 1) % 2][:, 0:3 * P], ACT.Copy)\
                     .then_inc(S("prT_ready"), 1)
            act_e.wait_ge(S("pr_T"), NH)
            act_e.wait_ge(S("o_mm"), NH - 2)
            a.activation(prT[:, (NH - 1) % 2, :], bank[5 + (NH - 1) % 2][:, 0:3 * P], ACT.Copy)\
             .then_inc(S("prT_ready"), 1)
            act_e.wait_ge(S("o_mm"), NH)
            for t in range(2):
                a.activation(fsq[:, 2 * t:2 * t + 2, :], bank[2 + t][:, :].rearrange("p (m t) -> p m t", m=2),
                             ACT.Square).then_inc(S("osq"), 1)
            a.activation(pf[:, 12:16, :], pf[:, 12:16, :], ACT.Sigmoid).then_inc(S("ogate"), 1)
            act_e.wait_ge(S("oms"), 1)
            a.activation(fsq[:, :, :], fsq[:, :, :], ACT.Sqrt).then_inc(S("orms"), 1)
            for cc in range(TT):
                act_e.wait_ge(S("mv_mm"), cc + 1)
                a.activation(MV[:, cc, :], bank[cc][:, :], ACT.Copy).then_inc(S("mv_ev"), 1)
            for s in range(4 * (len(LEVELS) - 1)):
                act_e.wait_ge(S("x_mm"), s + 1)
                if s >= 2:
                    act_e.wait_ge(S("tt_mm"), s - 1)
                a.activation(XT_[:, s % 2, :, :], bank[s % 2][:, :].rearrange("p (u t) -> p u t", u=4), ACT.Copy)\
                 .then_inc(S("x_ev"), 1)
            for n, dst in enumerate((TMV[:, 0, :], TMV[:, 1, :], TA[:, :])):
                act_e.wait_ge(S("tx_mm"), n + 1)
                a.activation(dst, bank[2 + n][:, :], ACT.Copy).then_inc(S("tx_ev"), 1)
            act_e.wait_ge(S("z_mm"), 1)
            a.activation(Z1[:, :, :], bank[5][:, 0:T].rearrange("p (m v) -> p m v", m=NF), ACT.Copy)\
             .then_inc(S("z_ev"), 1)
            for t in range(2):
                act_e.wait_ge(S("y_mm"), 2 + t)
                a.activation(yT[:, 2 * t:2 * t + 2, :], bank[t][:, :].rearrange("p (m t) -> p m t", m=2),
                             ACT.Copy).then_inc(S("yT_ready"), 1)
            act_e.wait_ge(S("yc_ready"), 1)
            a.activation(ysq[:, :, :], yT[:, :, :], ACT.Square).then_inc(S("ysq_ready"), 1)
            act_e.wait_ge(S("yms"), 1)
            a.activation(yrs[:, :, :], yrs[:, :, :], ACT.Sqrt).then_inc(S("yrms"), 1)
            for t in range(TT):
                act_e.wait_ge(S("x1_ready"), 3 + t)
                if t:
                    act_e.wait_ge(S("ss_ready"), TT + t)
                a.activation(x1q[:, :], x1[:, t, :], ACT.Square, accum_out=ss2[:, t:t + 1])\
                 .then_inc(S("ss_ready"), 1)
            act_e.wait_ge(S("ms_ready"), 2)
            a.activation(rs2[:, :], ss2[:, :], ACT.Sqrt).then_inc(S("rms_ready"), 1)
            for t in range(TT):
                act_e.wait_ge(S("h2_ready"), t + 1)
                a.activation(h_hi[:, t, :], h2[:, t, :], ACT.Copy).then_inc(S("hhi_ready"), 1)
            for n in range(4):
                act_e.wait_ge(S("h2_T"), n + 1)
                a.activation(h2T[:, 2 * n:2 * n + 2, :], bank[2 + n][:, :].rearrange("p (k t) -> p k t", k=2),
                             ACT.Copy).then_inc(S("h2T_ready"), 1)
            act_e.wait_ge(S("tdiff"), 1)
            a.activation(texp[:, :, :], texp[:, :, :], ACT.Exp).then_inc(S("texp_ready"), 1)
            act_e.wait_ge(S("gT_mm"), 1)
            a.activation(gT[:, :], bank[3][0:NE, 0:T], ACT.Copy).then_inc(S("gT_ready"), 1)

            def hi(i, cc, h):
                q = EC * i + cc
                if h == 0:
                    act_e.wait_ge(S(f"w_loaded{item_slot(cc)}"), item_loaded(cc)[1] + 16 * i)
                if not isinstance(i, int) or q >= 2:
                    act_e.wait_ge(S("half_mm"), 2 * q - 3 + h)
                a.activation(w_hi[:, cc % 2, 4 * h:4 * h + 4, :], raw[:, item_slot(cc), 4 * h:4 * h + 4, :],
                             ACT.Copy).then_inc(S("hi_ready"), 1)

            def take_acc(i, n):
                act_e.wait_ge(S("half_mm"), 2 * EC * i + 2 * min(n, 5) + 2 + 2 * (n == 4))
                looped = not isinstance(i, int)
                if n >= 3:
                    act_e.wait_ge(S("turned"), 4 * i + n - 2)
                elif n == 0 and looped:
                    act_e.wait_ge(S("turned"), 4 * i)
                elif looped:
                    act_e.wait_ge(S("scattered"), 2 * i - 2 + n)
                a.activation(evac[:, n % 3, :], bank[ACC[n]][:, :], ACT.Copy).then_inc(S("acc_ev"), 1)

            def take_xg(i, half):
                act_e.wait_ge(S("xg_mm"), 2 * i + half + 1)
                a.activation(xg[:, half * NC:(half + 1) * NC], bank[3][:, :], ACT.Copy).then_inc(S("xg_ready"), 1)

            def take_xT(i):
                act_e.wait_ge(S("xT_mm"), i + 1)
                a.activation(xT[:, :, 0, :], bank[3][:, :].rearrange("p (k c) -> p k c", k=KT), ACT.Copy)\
                 .then_inc(S("xThi_ready"), 1)

            def sigmoid(i, pair):
                act_e.wait_ge(S("gate_ready"), 2 * i + pair + 1)
                a.activation(sig[:, :, :], gated[:, :, :], ACT.Sigmoid, scale=ALPHA).then_inc(S("sig_ready"), 1)

            def act_hi(i, pair):
                act_e.wait_ge(S("act_ready"), 2 * i + pair + 1)
                a.activation(aT[:, 4 * pair:4 * pair + 4, 0, :], gated[:, :, :], ACT.Copy)\
                 .then_inc(S("aThi_ready"), 1)

            def item(i, first):
                hi(i, 0, 0)
                take_xT(i)
                hi(i, 0, 1)
                hi(i, 1, 0)
                if not first:
                    take_acc(i - 1, 4)
                    take_acc(i - 1, 5)
                hi(i, 1, 1)
                hi(i, 2, 0)
                take_acc(i, 0)
                hi(i, 2, 1)
                act_e.wait_ge(S("st_mm"), i + 1)
                a.activation(scat[:, :], bank[3][:, 0:T], ACT.Copy).then_inc(S("scat_ready"), 1)
                hi(i, 3, 0)
                take_acc(i, 1)
                sigmoid(i, 0)
                hi(i, 3, 1)
                hi(i, 4, 0)
                take_acc(i, 2)
                act_hi(i, 0)
                hi(i, 4, 1)
                take_xg(i + 1, 0)
                hi(i, 5, 0)
                take_acc(i, 3)
                hi(i, 5, 1)
                sigmoid(i, 1)
                take_xg(i + 1, 1)
                act_hi(i, 1)

            act_e.wait_ge(S("items_ready"), 2)
            n_it = act_e.value_load(n_items[0:1, 0:1], min_val=0, max_val=NI - NE) + NE
            act_e.wait_ge(S("moe_free"), 1)
            act_e.wait_ge(S("init_mm"), 1)
            act_e.wait_ge(S("x1_out"), 16)
            take_xg(0, 0)
            take_xg(0, 1)
            item(0, True)
            with act_e.Fori(1, n_it) as i:
                item(i, False)
            take_acc(n_it - 1, 4)
            take_acc(n_it - 1, 5)

            for t in range(TT):
                act_e.wait_ge(S("xo_ready"), t + 1)
                if t:
                    act_e.wait_ge(S("ss_ready"), 2 * TT + t)
                a.activation(yq[:, :], yo[:, t, :], ACT.Square, accum_out=ss3[:, t:t + 1])\
                 .then_inc(S("ss_ready"), 1)
            act_e.wait_ge(S("ms_ready"), 3)
            a.activation(rs3[:, :], ss3[:, :], ACT.Sqrt).then_inc(S("rms_ready"), 1)

        @block.vector
        def _(dve):
            v = nc.vector
            made = [0]

            def step(ins):
                made[0] += 1
                ins.then_inc(S("dve_step"), 1)
                dve.wait_ge(S("dve_step"), made[0])

            def ts(out_, in_, s1, s2, op0, op1=None):
                return v.tensor_scalar(out_, in_, s1, s2, op0, op1) if op1 is not None \
                    else v.tensor_scalar(out_, in_, s1, None, op0)

            def stt(out_, in0, s, in1, op0, op1):
                return v.scalar_tensor_tensor(out=out_, in0=in0, scalar=s, in1=in1, op0=op0, op1=op1)

            tt = v.tensor_tensor
            v.memset(pz[:, :, 0:1], 0.0)
            dve.wait_ge(S("rowsT"), 1)
            v.tensor_copy(colv[:, :], bank[5][:, 0:NROW]).then_inc(S("colv_ready"), 1)
            dve.wait_ge(S("colv_ready"), 1)
            step(ts(colof('q_norm_g'), colof('q_norm_g'), HD ** -0.5, None, ALU.mult))
            dve.wait_ge(S("ss_ready"), TT)
            ts(ss[:, :], ss[:, :], 1.0 / D, NORM_EPS, ALU.mult, ALU.add).then_inc(S("ms_ready"), 1)
            dve.wait_ge(S("rms_ready"), 1)
            step(v.reciprocal(rs[:, :], rs[:, :]))
            for t in range(TT):
                ts(x_sb[:, t, :], x_sb[:, t, :], rs[:, t:t + 1], None, ALU.mult).then_inc(S("xn_ready"), 1)
            dve.wait_ge(S("csig"), 1)
            step(tt(csil[:, :], csil[:, :], colof('c', 0, 8), ALU.mult))

            def ada(j):
                n = where[('ada', j)]
                dve.wait_ge(*loaded(n))
                dve.wait_ge(S("binit_in"), 16 * (j + 1))
                if j >= 2:
                    dve.wait_ge(S("acc_used"), j - 1)
                o = acc[:, j % 2, :]
                for k in range(KT):
                    i = stt(o, raw[:, slot_of(n), k, :], csil[:, k:k + 1], binit[:, :] if k == 0 else o,
                            ALU.mult, ALU.add)
                    if k == 0:
                        i.then_inc(S("binit_used"), 1)
                        dve.wait_ge(S("binit_used"), j + 1)
                    elif k < KT - 1:
                        step(i)
                    else:
                        i.then_inc(S("ada_used"), 1)

            for j in range(4):
                ada(j)
            dve.wait_ge(S("col_mm"), 1)
            v.tensor_copy(modc[:, 0:8], bank[4][:, 0:8])
            stt(modc[:, 8:16], bank[4][:, 8:16], 1.0, colof('norm1_g', 0, 8), ALU.add, ALU.mult)\
                .then_inc(S("modc_ready"), 1)

            def shift(j):
                tiles = range(4 * j, min(4 * j + 4, RT))
                n = len(tiles)
                dve.wait_ge(S("p_ev"), tiles[-1] + 1)
                step(tt(dtmp[:, 0:n, :], pz[:, 4 * j:4 * j + n, 0:T], pz[:, 4 * j:4 * j + n, 1:T + 1],
                        ALU.subtract))
                dst = (r_f, k_f, v_f, lora)[j]
                for t, m in enumerate(tiles):
                    i = stt(dst[:, t, :], dtmp[:, t, :], colof('mu_shift', m), pz[:, m, 1:T + 1],
                            ALU.mult, ALU.add)
                i.then_inc(S("shifted"), 1)

            for j in range(4):
                shift(j)
                ada(4 + j)
            ada(8)
            dve.wait_ge(S("shifted"), 4)
            dve.wait_ge(S("lora_ev"), 6)
            step(ts(logd[:, :, :], logd[:, :, :], -EXPM05, None, ALU.mult))
            for m in range(NF):
                i = ts(kk_f[:, m, :], k_f[:, m, :], colof('k_k', m), None, ALU.mult)
            step(i)
            tt(dtmp[:, :, :], kk_f[:, :, :], kk_f[:, :, :], ALU.mult).then_inc(S("kksq_ready"), 1)
            ada(9)
            dve.wait_ge(S("kknorm"), 2)
            step(ts(e_b[:, :, :], e_b[:, :, :], 1e-12, None, ALU.max))
            step(v.reciprocal(e_b[:, :, :], e_b[:, :, :]))
            step(tt(kk_f[:, :, :], kk_f[:, :, :], e_b[:, :, :], ALU.mult))
            for m in range(NF):
                i = ts(dtmp[:, m, :], a_f[:, m, :], -1.0, colof('k_a', m), ALU.add, ALU.mult)
            step(i)
            step(stt(k_f[:, :, :], dtmp[:, :, :], 1.0, k_f[:, :, :], ALU.add, ALU.mult))
            tt(b_f_[:, :, :], kk_f[:, :, :], a_f[:, :, :], ALU.mult)
            for m in range(NF):
                i = stt(dtmp[:, m, :], r_f[:, m, :], colof('r_k', m), k_f[:, m, :], ALU.mult, ALU.mult)
            i.then_inc(S("rkk_ready"), 1)
            ada(10)
            for m in range(NF):
                for cc in range(TT):
                    i = v.tensor_tensor_scan(cum[:, m, cc * P:(cc + 1) * P],
                                             ones[:, 0:P], logd[:, m, cc * P:(cc + 1) * P], 0.0,
                                             ALU.mult, ALU.add)
            step(i)
            dve.wait_ge(S("bon_mm"), 2)
            for t in range(2):
                tt(bonus[:, 2 * t:2 * t + 2, :], bank[5 + t][:, :].rearrange("p (m t) -> p m t", m=2),
                   v_f[:, 2 * t:2 * t + 2, :], ALU.mult).then_inc(S("bon_ev"), 1)
            cumc = cum[:, :, :].rearrange("p m (c t) -> p (m c) t", c=TT)
            d1c = dtmp[:, :, :].rearrange("p m (c t) -> p (m c) t", c=TT)
            tt(d1c, cumc, cumc[:, :, HD - 1:HD].to_broadcast([P, NF * TT, P]), ALU.subtract)\
                .then_inc(S("d1_ready"), 1)
            r_c = r_f[:, :, :].rearrange("p m (c t) -> p m c t", c=TT)
            k_c, b_c, kk_c, e_ac, e_bc = (y[:, :, :].rearrange("p m (c t) -> p m c t", c=TT)
                                          for y in (k_f, b_f_, kk_f, e_a, e_b))
            dve.wait_ge(S("exps"), 2)
            tt(AR[:, :, :, 1, :], r_c, e_ac, ALU.mult)
            tt(Kr[:, :, :, :], k_c, e_bc, ALU.mult)
            stt(nBr[:, :, :, :].rearrange("p m c t -> p (m c t)"), b_f_[:, :, :].rearrange("p m t -> p (m t)"), -1.0,
                e_b[:, :, :].rearrange("p m t -> p (m t)"), ALU.mult, ALU.mult)
            dve.wait_ge(S("d1_ready"), 1)
            tt(dtmp[:, :, :], dtmp[:, :, :], logd[:, :, :], ALU.subtract).then_inc(S("d2_ready"), 1)
            ada(11)
            dve.wait_ge(S("exps"), 3)
            tt(AR[:, :, :, 0, :], kk_c, e_ac, ALU.mult).then_inc(S("A_ready"), 1)
            dve.wait_ge(S("A_ready"), 1)
            tt(e_a[:, :, P:T], cum[:, :, P:T], logd[:, :, P:T], ALU.subtract).then_inc(S("d3_ready"), 1)
            dlast = dtmp[:, 0:2, :].rearrange("p m (h t) -> p (m h) t", h=2)
            tt(dlast, cum[:, :, 0:P], cum[:, :, P - 1:P].to_broadcast([P, NF, P]), ALU.subtract)\
                .then_inc(S("d4_ready"), 1)
            dve.wait_ge(S("exps"), 5)
            dve.wait_ge(S("acc_used"), NADA)
            dve.wait_ge(S("mod_out"), 16 * 8)
            tt(R0[:, :, :], r_f[:, :, P:T], e_b[:, :, 0:P], ALU.mult)
            tt(A0[:, :, :], kk_f[:, :, P:T], e_a[:, :, 0:P], ALU.mult).then_inc(S("tm_src"), 1)
            dve.wait_ge(S("exps"), 6)
            tt(Kb[:, :, :], k_f[:, :, 0:P], e_b[:, :, P:T], ALU.mult).then_inc(S("tm_src"), 1)
            stt(nBb[:, :, :], b_f_[:, :, 0:P], -1.0, e_b[:, :, P:T], ALU.mult, ALU.mult)\
                .then_inc(S("tm_src"), 1)
            dve.wait_ge(S("p_ev"), INT)
            step(ts(ncum[:, :], fz[:, :], -1.0, None, ALU.mult))
            tt(ncum[:, :], ncum[:, :], fz[:, :], ALU.min).then_inc(S("fabs"), 1)
            dve.wait_ge(S("tm_src"), 3)
            dve.wait_ge(S("bon_ev"), 2)
            v.memset(rinv[:, :, :], 0.0).then_inc(S("ew_done"), 1)
            dve.wait_ge(S("fln"), 1)
            step(stt(fz[:, :], fz[:, :], 0.0, ncum[:, :], ALU.min, ALU.subtract))
            v.tensor_tensor_scan(ncum[:, :], ones[0:NH, 0:1].to_broadcast([NH, T]), fz[:, :], 0.0,
                                 ALU.mult, ALU.subtract).then_inc(S("ncum_ready"), 1)
            dve.wait_ge(S("tm_T"), 5)
            for n, name in enumerate(('q_norm_g', 'k_norm_g')):
                w = pf[:, 4 * n:4 * n + 4, :]
                tt(fsq[:, :, :], w, w, ALU.mult).then_inc(S("fsq_ready"), 1)
                dve.wait_ge(S("fsum_mm"), 2 * n + 2)
                for t in range(2):
                    i = ts(fsq[:, 2 * t:2 * t + 2, :], bank[2 + t][:, :].rearrange("p (m t) -> p m t", m=2),
                           1.0 / HD, NORM_EPS, ALU.mult, ALU.add)
                i.then_inc(S("fms"), 1)
                dve.wait_ge(S("frms"), n + 1)
                step(v.reciprocal(fsq[:, :, :], fsq[:, :, :]))
                i = stt(w, w, colof(name), fsq[:, :, :], ALU.mult, ALU.mult)
                i.then_inc(S("qk_ready"), 1)
                dve.wait_ge(S("qk_ready"), n + 1)
            for h in range(NH):
                dve.wait_ge(S("s_mm"), h + 1)
                if h >= 2:
                    dve.wait_ge(S("pr_T"), h - 1)
                b = bank[h % 2]
                p_h = pr[:, h % 2, :]
                tt(p_h[:, 0:P], b[:, 0:P], causal[:, :], ALU.add)
                tt(p_h[:, 2 * P:3 * P], b[:, 2 * P:3 * P], causal[:, :], ALU.add)
                v.tensor_copy(p_h[:, P:2 * P], b[:, P:2 * P]).then_inc(S("s_ev"), 1)
                dve.wait_ge(S("s_ev"), h + 1)
                v.tensor_reduce(rmax[:, h % 2, 0:1], p_h[:, 0:P], AX.X, ALU.max)
                step(v.tensor_reduce(rmax[:, h % 2, 1:2], p_h[:, P:3 * P], AX.X, ALU.max))
                ts(rmax[:, h % 2, :], rmax[:, h % 2, :], -1.0, None, ALU.mult).then_inc(S("smax"), 1)
                dve.wait_ge(S("sexp"), h + 1)
                step(v.reciprocal(rinv[:, h % 2, :], rsum[:, h % 2, :]))
                ts(p_h[:, 0:P], p_h[:, 0:P], rinv[:, h % 2, 0:1], None, ALU.mult)
                ts(p_h[:, P:3 * P], p_h[:, P:3 * P], rinv[:, h % 2, 1:2], None, ALU.mult)\
                    .then_inc(S("pr_ready"), 1)
            dve.wait_ge(S("osum_mm"), 2)
            for t in range(2):
                i = ts(fsq[:, 2 * t:2 * t + 2, :], bank[t][:, :].rearrange("p (m t) -> p m t", m=2),
                       1.0 / HD, NORM_EPS, ALU.mult, ALU.add)
            i.then_inc(S("oms"), 1)
            dve.wait_ge(S("orms"), 1)
            step(v.reciprocal(fsq[:, :, :], fsq[:, :, :]))
            for t in range(2):
                i = tt(mix_f[:, 2 * t:2 * t + 2, :], bank[2 + t][:, :].rearrange("p (m t) -> p m t", m=2),
                       fsq[:, 2 * t:2 * t + 2, :], ALU.mult)
            step(i)
            dve.wait_ge(S("ogate"), 1)
            stt(mix_f[:, :, :], mix_f[:, :, :], colof('o_norm_g'), pf[:, 12:16, :], ALU.mult, ALU.mult)\
                .then_inc(S("mixf_ready"), 1)
            dve.wait_ge(S("LR_zero"), 1)
            for u in range(NU):
                dve.wait_ge(S("lr_mm"), u + 1)
                b = bank[4 + u % 4][:, :].rearrange("p (a b t) -> p a (b t)", a=2, b=2)
                v.copy_predicated(LR[:, u, :, :].rearrange("p (a b) t -> p a (b t)", a=2),
                                  lrmask[:, :, :].rearrange("p b t -> p (b t)").unsqueeze(1).to_broadcast([P, 2, 2 * P]),
                                  b).then_inc(S("lr_ev"), 1)
            dve.wait_ge(S("T_ident"), 2)
            dve.wait_ge(S("lr_ev"), NU)
            for g in range(4):
                dve.wait_ge(S("nL_T"), g + 1)
                us = slice(4 * g, 4 * g + 4)
                v.copy_predicated(Ti[:, us, :], lev[:, 0:1, :].to_broadcast([P, 4, P]),
                                  bank[g][:, :].rearrange("p (u t) -> p u t", u=4))
                v.copy_predicated(TiT[:, us, :], levT[:, 0:1, :].to_broadcast([P, 4, P]), LR[:, us, 0, :])\
                    .then_inc(S("T_up"), 1)
            for s in range(4 * (len(LEVELS) - 1)):
                n, g = 1 + s // 4, s % 4
                us = slice(4 * g, 4 * g + 4)
                dve.wait_ge(S("tt_mm"), s + 1)
                if n < len(LEVELS) - 1:
                    v.copy_predicated(Ti[:, us, :], lev[:, n:n + 1, :].to_broadcast([P, 4, P]),
                                      bank[2 + 2 * (s % 2)][:, :].rearrange("p (u t) -> p u t", u=4))
                v.copy_predicated(TiT[:, us, :], levT[:, n:n + 1, :].to_broadcast([P, 4, P]),
                                  bank[3 + 2 * (s % 2)][:, :].rearrange("p (u t) -> p u t", u=4))\
                    .then_inc(S("T_up"), 1)
            dve.wait_ge(S("q_mm"), 1)
            tt(QT[:, :, :], bank[6][:, :].rearrange("p (m t) -> p m t", m=NF), R0[:, :, :], ALU.add)\
                .then_inc(S("QT_ready"), 1)
            dve.wait_ge(S("ymean_mm"), 2)
            for t in range(2):
                i = stt(yT[:, 2 * t:2 * t + 2, :], bank[2 + t][:, :].rearrange("p (m t) -> p m t", m=2), -1.0 / HD,
                        yT[:, 2 * t:2 * t + 2, :], ALU.mult, ALU.add)
            i.then_inc(S("yc_ready"), 1)
            dve.wait_ge(S("yvar_mm"), 2)
            for t in range(2):
                i = ts(yrs[:, 2 * t:2 * t + 2, :], bank[4 + t][:, :].rearrange("p (m t) -> p m t", m=2),
                       1.0 / HD, GN_EPS, ALU.mult, ALU.add)
            i.then_inc(S("yms"), 1)
            dve.wait_ge(S("yrms"), 1)
            step(v.reciprocal(yrs[:, :, :], yrs[:, :, :]))
            step(tt(yT[:, :, :], yT[:, :, :], yrs[:, :, :], ALU.mult))
            for m in range(NF):
                i = ts(yT[:, m, :], yT[:, m, :], colof('gn_w', m), colof('gn_b', m), ALU.mult, ALU.add)
            step(i)
            step(tt(yT[:, :, :], yT[:, :, :], bonus[:, :, :], ALU.add))
            tt(mix_r[:, :, :], yT[:, :, :], g_f[:, :, :], ALU.mult).then_inc(S("mixr_ready"), 1)
            dve.wait_ge(S("late_in"), 16 * 5)
            step(stt(scale2[:, :], scale2[:, :], 1.0, n2g[:, :], ALU.add, ALU.mult))
            for j in range(NOUT):
                for t in range(TT):
                    n = 2 * j + t
                    cols = slice(j * NC, (j + 1) * NC)
                    dve.wait_ge(S("wo_mm"), n + 1)
                    step(tt(evac[:, t, :], bank[(6, 7, 0, 1)[n]][:, :], gate1[:, cols], ALU.mult))
                    tt(x1[:, t, cols], x1[:, t, cols], evac[:, t, :], ALU.add).then_inc(S("x1_ready"), 1)
            dve.wait_ge(S("ss_ready"), 2 * TT)
            ts(ss2[:, :], ss2[:, :], 1.0 / D, NORM_EPS, ALU.mult, ALU.add).then_inc(S("ms_ready"), 1)
            dve.wait_ge(S("rms_ready"), 2)
            step(v.reciprocal(rs2[:, :], rs2[:, :]))
            for t in range(TT):
                step(stt(h2[:, t, :], x1[:, t, :], rs2[:, t:t + 1], scale2[:, :], ALU.mult, ALU.mult))
                tt(h2[:, t, :], h2[:, t, :], shift2[:, :], ALU.add).then_inc(S("h2_ready"), 1)
            for t in range(TT):
                dve.wait_ge(S("h2_ready"), t + 1)
                dve.wait_ge(S("hhi_ready"), t + 1)
                tt(h_lo[:, t, :], h2[:, t, :], h_hi[:, t, :].bitcast(F32), ALU.subtract).then_inc(S("hlo_ready"), 1)
            dve.wait_ge(S("bias_T"), 1)
            bT = bank[7][:, :].rearrange("p (s e) -> p s e", e=NE)
            for cc in range(4):
                tile0 = (0, 8, 4, 12)[cc]
                i = ts(biasT[:, :, cc, :].rearrange("p e s -> p s e"), bT[:, tile0:tile0 + 4, :], float(cc % 2),
                       None, ALU.add)
            i.then_inc(S("biasT_ready"), 1)
            dve.wait_ge(S("late2_in"), 16 * 4)
            dve.wait_ge(S("late_consts"), 2)
            dve.wait_ge(S("router_mm"), 1)
            step(tt(logits[:, :, :], bank[6][:, 0:TT * NE].rearrange("p (t e) -> p t e", t=TT),
                    brt[:, :].unsqueeze(1).to_broadcast([P, TT, NE]), ALU.add))
            for t in range(TT):
                i = v.max(top8[:, t, :], logits[:, t, :])
            step(i)
            for t in range(TT):
                i = v.max_index(idx8[:, t, :], top8[:, t, :], logits[:, t, :])
            step(i)
            v.tensor_copy(idxf[:, :, :], idx8[:, :, :])
            tt(texp[:, :, :], top8[:, :, 0:TOPK], top8[:, :, 0:1].to_broadcast([P, TT, TOPK]), ALU.subtract)\
                .then_inc(S("tdiff"), 1)
            dve.wait_ge(S("texp_ready"), 1)
            step(v.tensor_reduce(tsum[:, :], texp[:, :, :], AX.X, ALU.add))
            step(v.reciprocal(tsum[:, :], tsum[:, :]))
            step(tt(texp[:, :, :], texp[:, :, :], tsum[:, :].unsqueeze(2).to_broadcast([P, TT, TOPK]), ALU.mult))
            for t in range(TT):
                for k in range(TOPK):
                    i = ts(gk[:, t, k, :], iota_e[:, :], idxf[:, t, k:k + 1], texp[:, t, k:k + 1],
                           ALU.is_equal, ALU.mult)
            step(i)
            step(v.tensor_reduce(gates[:, :, :], gk[:, :, :, :].rearrange("p t k e -> p t e k"), AX.X, ALU.add))
            ts(sel[:, :, :], gates[:, :, :], 0.0, None, ALU.is_gt).then_inc(S("sel_ready"), 1)
            dve.wait_ge(S("rank_mm"), 1)
            step(v.tensor_copy(cnt[:, :], bank[2][:, 2 * NE:3 * NE]))
            for j in range(4):
                i = ts(ge[:, j, :], cnt[:, :], float(CAP * j), None, ALU.is_gt if j else ALU.is_ge)
            step(i)
            step(v.tensor_reduce(nblk[:, :], ge[:, :, :].rearrange("p j e -> p e j"), AX.X, ALU.add))
            step(v.tensor_tensor_scan(binc[:, :], ones[:, 0:NE], nblk[:, :], 0.0, ALU.mult, ALU.add))
            step(tt(bexc[:, :], binc[:, :], nblk[:, :], ALU.subtract))
            step(ts(bexc[:, :], bexc[:, :], float(CAP), None, ALU.mult))
            step(tt(pos[:, :, :], bank[2][:, 0:TT * NE].rearrange("p (t e) -> p t e", t=TT),
                    bexc[:, :].unsqueeze(1).to_broadcast([P, TT, NE]), ALU.add))
            step(stt(pos[:, :, :], pos[:, :, :], 1.0, sel[:, :, :], ALU.add, ALU.mult))
            step(ts(pos[:, :, :], pos[:, :, :], -1.0, None, ALU.add))
            step(tt(icmp[:, :, :], binc[0:1, :].unsqueeze(1).to_broadcast([1, NI + 2, NE]),
                    iota_i[:, :].unsqueeze(2).to_broadcast([1, NI + 2, NE]), ALU.is_le))
            step(v.tensor_reduce(isum[:, :], icmp[:, :, :], AX.X, ALU.add))
            ts(items[:, :], isum[:, :], float(NE - 1), None, ALU.min).then_inc(S("items_ready"), 1)
            ts(n_items[:, :], binc[0:1, NE - 1:NE].to_broadcast([1, 2]), float(-NE), None, ALU.add).then_inc(S("items_ready"), 1)
            dve.wait_ge(S("items_ready"), 2)
            dve.wait_ge(S("biasT_ready"), 1)
            v.memset(ss2[:, :], 0.0).then_inc(S("moe_free"), 1)

            K = 10

            class Body:

                def __init__(self, i):
                    self.i, self.n = i, 0

                def step(self, ins):
                    self.n += 1
                    ins.then_inc(S("item_step"), 1)
                    dve.wait_ge(S("item_step"), self.i * K + self.n)

            def lo(i, cc, h):
                dve.wait_ge(S("hi_ready"), 2 * (EC * i + cc) + h + 1)
                part = slice(4 * h, 4 * h + 4)
                tt(w_lo[:, cc % 2, part, :], raw[:, item_slot(cc), part, :],
                   w_hi[:, cc % 2, part, :].bitcast(F32), ALU.subtract).then_inc(S("lo_ready"), 1)

            def select(i):
                e_i = dve.value_load(items[0:1, bass.ds(i, 1)], min_val=0, max_val=NE - 1)
                for t in range(TT):
                    ts(onehot[:, t, :, :], slots[:, :, :], pos[:, t, bass.ds(e_i, 1)], None, ALU.is_equal)
                    i2 = ts(gatehot[:, t, :, :], slots[:, :, :], pos[:, t, bass.ds(e_i, 1)],
                            gates[:, t, bass.ds(e_i, 1)], ALU.is_equal, ALU.mult)
                i2.then_inc(S("onehot_ready"), 1)

            def join(dst, cc, body):
                b = bank[ACC[cc]][:, :].rearrange("p (s a c) -> p s a c", s=4, a=2)
                body.step(tt(dst[:, :, :], b[:, :, 0, :], bias_i[:, cc, :].unsqueeze(2).to_broadcast([P, 4, CAP]),
                             ALU.add))
                tt(dst[:, :, :], b[:, :, 1, :], dst[:, :, :], ALU.add).then_inc(S("tr_ev"), 1)

            def gate(i, pair, body):
                dve.wait_ge(S("turned"), 4 * i + 2 * pair + 1)
                dve.wait_ge(S("aT_ready"), 2 * i + pair) if not isinstance(i, int) or pair else None
                join(gated, 2 * pair, body)
                dve.wait_ge(S("tr_ev"), 4 * i + 2 * pair + 1)
                ts(gated[:, :, :], gated[:, :, :], LIMIT, None, ALU.min).then_inc(S("gate_ready"), 1)

            def up(i, pair, body):
                dve.wait_ge(S("turned"), 4 * i + 2 * pair + 2)
                join(ups, 2 * pair + 1, body)
                dve.wait_ge(S("tr_ev"), 4 * i + 2 * pair + 2)
                body.step(ts(ups[:, :, :], ups[:, :, :], 1.0 - LIMIT, 1.0 + LIMIT, ALU.max, ALU.min))
                dve.wait_ge(S("sig_ready"), 2 * i + pair + 1)
                body.step(tt(gated[:, :, :], gated[:, :, :], sig[:, :, :], ALU.mult))
                tt(gated[:, :, :], gated[:, :, :], ups[:, :, :], ALU.mult).then_inc(S("act_ready"), 1)

            def act_lo(i, pair):
                dve.wait_ge(S("aThi_ready"), 2 * i + pair + 1)
                part = slice(4 * pair, 4 * pair + 4)
                tt(aT[:, part, 1, :], gated[:, :, :], aT[:, part, 0, :].bitcast(F32), ALU.subtract)\
                    .then_inc(S("aT_ready"), 1)

            def take_xT(i):
                dve.wait_ge(S("xThi_ready"), i + 1)
                tt(xT[:, :, 1, :], bank[3][:, :].rearrange("p (k c) -> p k c", k=KT),
                   xT[:, :, 0, :].bitcast(F32), ALU.subtract).then_inc(S("xT_ready"), 1)

            def item(i):
                body = Body(i)
                lo(i, 0, 0)
                lo(i, 0, 1)
                take_xT(i)
                lo(i, 1, 0)
                e = dve.value_load(items[0:1, bass.ds(i, 1)], min_val=0, max_val=NE - 1)
                body.step(v.tensor_copy(bias_i[:, :, :].rearrange("p c s -> p (c s)"),
                                        biasT[:, bass.ds(e, 1), :, :].rearrange("p e c s -> p (e c s)")))
                lo(i, 1, 1)
                lo(i, 2, 0)
                gate(i, 0, body)
                lo(i, 2, 1)
                dve.wait_ge(S("st_mm"), i + 1)
                body.step(ts(slots[:, :, :], slots[:, :, :], float(CAP), None, ALU.add))
                select(i + 1)
                lo(i, 3, 0)
                up(i, 0, body)
                lo(i, 3, 1)
                lo(i, 4, 0)
                act_lo(i, 0)
                gate(i, 1, body)
                lo(i, 4, 1)
                lo(i, 5, 0)
                up(i, 1, body)
                lo(i, 5, 1)
                act_lo(i, 1)
                assert body.n == K

            n_it = dve.value_load(n_items[0:1, 0:1], min_val=0, max_val=NI - NE) + NE
            select(0)
            item(0)
            with dve.Fori(1, n_it) as i:
                item(i)

            dve.wait_ge(S("end_in"), 16 * 3)
            dve.wait_ge(S("scattered"), 2 * n_it)
            for t in range(TT):
                for half in range(NOUT):
                    cols = slice(half * NC, (half + 1) * NC)
                    i = tt(yo[:, t, cols], bank[4 + 2 * t + half][:, :], gate2[:, cols], ALU.mult)
                step(i)
                tt(yo[:, t, :], yo[:, t, :], x1e[:, t * D:(t + 1) * D], ALU.add).then_inc(S("xo_ready"), 1)
            dve.wait_ge(S("ss_ready"), 3 * TT)
            ts(ss3[:, :], ss3[:, :], 1.0 / D, NORM_EPS, ALU.mult, ALU.add).then_inc(S("ms_ready"), 1)
            dve.wait_ge(S("rms_ready"), 3)
            step(v.reciprocal(rs3[:, :], rs3[:, :]))
            for t in range(TT):
                stt(yo[:, t, :], yo[:, t, :], rs3[:, t:t + 1], fg, ALU.mult, ALU.mult).then_inc(S("out_ready"), 1)

        @block.tensor
        def _(pe):
            mm, tr = nc.tensor.matmul, nc.tensor.transpose
            pe.wait_ge(S("consts"), 1)
            pe.wait_ge(S("rows_in"), 16 * NROWDMA)
            tr(bank[5][:, 0:NROW], rowv[:, :], ident[0:NROW, 0:NROW]).then_inc(S("rowsT"), 1)
            for k in range(KT):
                for t in range(TT):
                    pe.wait_ge(S("xn_ready"), t + 1)
                    i = tr(bank[k // 2][:, (k % 2) * T + t * P:(k % 2) * T + (t + 1) * P],
                           x_sb[:, t, k * P:(k + 1) * P], ident[:, :])
                if k % 2:
                    i.then_inc(S("xnT"), 1)
            for j in range(4):
                pe.wait_ge(S("ada_used"), j + 1)
                for s in range(4):
                    i = mm(bank[4][:, 4 * j + s:4 * j + s + 1], acc[:, j % 2, s * P:(s + 1) * P], ones[:, 0:1],
                           start=True, stop=True)
                i.then_inc(S("acc_used"), 1)
            mm(bank[4][:, 16:17], ident[:, :], ones[:, 0:1], start=True, stop=True).then_inc(S("col_mm"), 1)

            def project(m):
                n = where[('in', m // 4)]
                pe.wait_ge(*loaded(n))
                if m >= 4:
                    pe.wait_ge(S("p_ev"), m - 3)
                else:
                    pe.wait_ge(S("hT_ready"), KT)
                w = P if m < INT - 1 else NH
                for k in range(KT):
                    i = mm(bank[m % 4][0:w, 0:T], raw[:, slot_of(n), k, (m % 4) * P:(m % 4) * P + w], hT[:, k, :],
                           start=(k == 0), stop=(k == KT - 1))
                i.then_inc(S("p_mm"), 1)

            def mod_row(j):
                pe.wait_ge(S("ada_used"), 5 + j)
                if j:
                    pe.wait_ge(S("arow_ready"), j)
                else:
                    pe.wait_ge(S("modc_ready"), 1)
                mm(bank[4][0:1, :], ones[:, 0:1], acc[:, j % 2, :], start=True, stop=True)\
                    .then_inc(S("acc_used"), 1)

            def head_sums(src, banks, done, acc_=None):
                for t in range(2):
                    mm(bank[banks[t]][:, :], blk[:, :], src[:, 2 * t:2 * t + 2, :].rearrange("p m t -> p (m t)"),
                       start=True, stop=True).then_inc(S(done), 1)

            for m in range(16):
                project(m)
                if m in (7, 11, 15):
                    mod_row((m - 7) // 4)
            project(16)
            project(17)
            pe.wait_ge(S("lora_act"), 1)
            pe.wait_ge(S("lora_in"), 16 * 3)
            for q in range(6):
                if q >= 3:
                    pe.wait_ge(S("lora_ev"), q - 2)
                for t in range(2):
                    m = 2 * (q % 2) + t
                    o = bank[5 + q % 3][:, t * T:(t + 1) * T]
                    cols = slice(m * P, (m + 1) * P)
                    if q < 2:
                        i = mm(o, lora_w[0:HD, cols], loraa[0:HD, 0, :], start=True, stop=True)
                    elif q < 4:
                        i = mm(o, lora_w[HD:P, cols], loraa[HD:P, 0, :], start=True, stop=True)
                    else:
                        i = mm(o, g2_sb[:, cols], loraa[:, 1, :], start=True, stop=True)
                i.then_inc(S("lora_mm"), 1)
            for m in range(18, 20):
                project(m)
            mod_row(3)
            pe.wait_ge(S("kksq_ready"), 1)
            pe.wait_ge(S("lora_ev"), 6)
            head_sums(dtmp, (5, 6), "kksum_mm")
            for m in range(20, 24):
                project(m)
            mod_row(4)
            pe.wait_ge(S("rkk_ready"), 1)
            pe.wait_ge(S("kknorm"), 2)
            head_sums(dtmp, (5, 6), "bon_mm")
            for m in range(24, 28):
                project(m)
            mod_row(5)
            for m in range(28, INT):
                project(m)
            mod_row(6)
            mod_row(7)
            pe.wait_ge(S("shifted"), 3)
            pe.wait_ge(S("bon_ev"), 2)
            for t in range(TT):
                for m in range(NF):
                    i = tr(bank[5 + t][:, m * P:(m + 1) * P], v_f[:, m, t * P:(t + 1) * P], ident[:, :])
                i.then_inc(S("tm_T"), 1)
            pe.wait_ge(S("p_ev"), INT)
            for n, (src, b) in enumerate(((A0, 7), (Kb, 0), (nBb, 1))):
                pe.wait_ge(S("tm_src"), n + 1)
                for m in range(NF):
                    i = tr(bank[b][:, m * P:(m + 1) * P], src[:, m, :], ident[:, :])
                i.then_inc(S("tm_T"), 1)
            pe.wait_ge(S("fsq_ready"), 1)
            head_sums(fsq, (2, 3), "fsum_mm")
            pe.wait_ge(S("fsq_ready"), 2)
            head_sums(fsq, (2, 3), "fsum_mm")
            pe.wait_ge(S("tm_ev"), 5)
            for t in range(TT):
                for m in range(NF):
                    i = tr(bank[5 + t][:, m * P:(m + 1) * P], pf[:, 8 + m, t * P:(t + 1) * P], ident[:, :])
                i.then_inc(S("fv_T"), 1)
            pe.wait_ge(S("ncum_ready"), 1)
            pe.wait_ge(S("qk_ready"), 2)

            def scores(h):
                m, rows = tile_of(h)
                if h >= 2:
                    pe.wait_ge(S("s_ev"), h - 1)
                for t in range(TT):
                    n = (t + 1) * P
                    o = bank[h % 2][:, t * P:t * P + n]
                    mm(o, pf[rows, m, t * P:(t + 1) * P], pf[rows, 4 + m, 0:n], start=True, stop=False)
                    i = mm(o, ident[0:NH, h:h + 1].to_broadcast([NH, P]), ncum[:, 0:n], start=False, stop=True)
                i.then_inc(S("s_mm"), 1)

            def attend(h):
                m, rows = tile_of(h)
                pe.wait_ge(S("pr_ready"), h + 1)
                if h >= 2:
                    pe.wait_ge(S("prT_ready"), h - 1)
                else:
                    pe.wait_ge(S("fv_ev"), TT)
                for b in range(3):
                    i = tr(bank[5 + h % 2][:, b * P:(b + 1) * P], pr[:, h % 2, b * P:(b + 1) * P], ident[:, :])
                i.then_inc(S("pr_T"), 1)
                pe.wait_ge(S("prT_ready"), h + 1)
                vcols = slice(h * HD, (h + 1) * HD)
                o = bank[2 + m // 2][rows, (m % 2) * T:(m % 2) * T + T]
                mm(o[:, 0:P], fvt[:, 0, vcols], prT[:, h % 2, 0:P], start=True, stop=True)
                mm(o[:, P:T], fvt[:, 0, vcols], prT[:, h % 2, P:2 * P], start=True, stop=False)
                mm(o[:, P:T], fvt[:, 1, vcols], prT[:, h % 2, 2 * P:3 * P], start=False, stop=True)\
                    .then_inc(S("o_mm"), 1)

            scores(0)
            for h in range(NH):
                if h + 1 < NH:
                    scores(h + 1)
                attend(h)
            pe.wait_ge(S("osq"), 2)
            pe.wait_ge(S("s_ev"), NH)
            head_sums(fsq, (0, 1), "osum_mm")
            for u in range(NU):
                cc, (m, rows) = u // NH, tile_of(u % NH)
                b = bank[4 + u % 4]
                if u >= 4:
                    pe.wait_ge(S("lr_ev"), u - 3)
                ar = AR[rows, m, cc, :, :].rearrange("p b t -> p (b t)")
                mm(b[:, 0:2 * P], nBr[rows, m, cc, :], ar, start=True, stop=True)
                mm(b[:, 2 * P:4 * P], Kr[rows, m, cc, :], ar, start=True, stop=True).then_inc(S("lr_mm"), 1)
            pe.wait_ge(S("lr_ev"), NU)
            pe.wait_ge(S("oms"), 1)
            for u in range(NU):
                cc, h = u // NH, u % NH
                i = mm(bank[cc][:, h * HD:(h + 1) * HD], LR[:, u, 2, :], Vt[:, cc, h * HD:(h + 1) * HD],
                       start=True, stop=True)
                if h == NH - 1:
                    i.then_inc(S("mv_mm"), 1)
            pe.wait_ge(S("mv_ev"), TT)
            pe.wait_ge(S("mixf_ready"), 1)
            for g in range(4):
                for n in range(4):
                    i = tr(bank[g][:, n * P:(n + 1) * P], LR[:, 4 * g + n, 0, :], ident[:, :])
                i.then_inc(S("nL_T"), 1)

            def level_x(s):
                g = s % 4
                pe.wait_ge(S("T_up"), s + 1)
                if s < 2:
                    pe.wait_ge(S("T_up"), 4)
                else:
                    pe.wait_ge(S("x_ev"), s - 1)
                for n in range(4):
                    u = 4 * g + n
                    i = mm(bank[s % 2][:, n * P:(n + 1) * P], LR[:, u, 0, :], Ti[:, u, :], start=True, stop=True)
                i.then_inc(S("x_mm"), 1)

            def level_t(s):
                g, two = s % 4, s < 4 * (len(LEVELS) - 2)
                pe.wait_ge(S("x_ev"), s + 1)
                if s >= 2:
                    pe.wait_ge(S("T_up"), 4 + s - 1)
                for n in range(4):
                    u = 4 * g + n
                    if two:
                        mm(bank[2 + 2 * (s % 2)][:, n * P:(n + 1) * P], TiT[:, u, :], XT_[:, s % 2, n, :],
                           start=True, stop=True)
                    i = mm(bank[3 + 2 * (s % 2)][:, n * P:(n + 1) * P], XT_[:, s % 2, n, :], TiT[:, u, :],
                           start=True, stop=True)
                i.then_inc(S("tt_mm"), 1)

            steps = 4 * (len(LEVELS) - 1)
            level_x(0)
            for s in range(steps):
                if s + 1 < steps:
                    level_x(s + 1)
                level_t(s)
            pe.wait_ge(S("T_up"), 4 + steps)
            for n, (cc, rhs) in enumerate(((0, MV[:, 0, :]), (1, MV[:, 1, :]), (1, A0t[:, :]))):
                for h in range(NH):
                    i = mm(bank[2 + n][:, h * HD:(h + 1) * HD], TiT[:, cc * NH + h, :], rhs[:, h * HD:(h + 1) * HD],
                           start=True, stop=True)
                i.then_inc(S("tx_mm"), 1)

            def outputs(u, last_):
                cc, h = u // NH, u % NH
                m, rows = tile_of(h)
                vcols = slice(h * HD, (h + 1) * HD)
                o = bank[m // 2][rows, (m % 2) * T + cc * P:(m % 2) * T + (cc + 1) * P]
                mm(o, Vt[:, cc, vcols], LR[:, u, 3, :], start=True, stop=False)
                return mm(o, TMV[:, cc, vcols], LR[:, u, 1, :], start=False, stop=last_), o

            pe.wait_ge(S("tx_ev"), 1)
            for h in range(NH):
                m, rows = tile_of(h)
                vcols = slice(h * HD, (h + 1) * HD)
                o = bank[5][rows, m * HD:(m + 1) * HD]
                mm(o, Kbt[:, vcols], Vt[:, 0, vcols], start=True, stop=False)
                i = mm(o, nBbt[:, vcols], TMV[:, 0, vcols], start=False, stop=True)
            i.then_inc(S("z_mm"), 1)
            pe.wait_ge(S("tx_ev"), 3)
            for h in range(NH):
                m, rows = tile_of(h)
                i = mm(bank[6][rows, m * P:(m + 1) * P], TA[:, h * HD:(h + 1) * HD], LR[:, NH + h, 1, :],
                       start=True, stop=True)
            i.then_inc(S("q_mm"), 1)
            for u in range(NH):
                i, _ = outputs(u, True)
            i.then_inc(S("y_mm"), 1)
            pe.wait_ge(S("QT_ready"), 1)
            pe.wait_ge(S("z_ev"), 1)
            for u in range(NH, NU):
                m, rows = tile_of(u % NH)
                _, o = outputs(u, False)
                i = mm(o, Z1[rows, m, :], QT[rows, m, :], start=False, stop=True)
                if u % 4 == 3:
                    i.then_inc(S("y_mm"), 1)
            pe.wait_ge(S("yT_ready"), 2)
            head_sums(yT, (2, 3), "ymean_mm")
            pe.wait_ge(S("ysq_ready"), 1)
            head_sums(ysq, (4, 5), "yvar_mm")
            for j in range(NOUT):
                n = where[('out', j)]
                pe.wait_ge(*loaded(n))
                for t in range(TT):
                    o = bank[(6, 7, 0, 1)[2 * j + t]]
                    for n_k, k in enumerate((4, 5, 6, 7, 0, 1, 2, 3)):
                        if k == 0:
                            pe.wait_ge(S("mixr_ready"), 1)
                        src = mix_f[:, k - 4, t * P:(t + 1) * P] if k >= 4 else mix_r[:, k, t * P:(t + 1) * P]
                        i = mm(o[:, :], src, raw[:, slot_of(n), k, :], start=(n_k == 0), stop=(n_k == 7))
                    i.then_inc(S("wo_mm"), 1)
            pe.wait_ge(S("late2_in"), 16 * 4)
            pe.wait_ge(S("x1_ready"), 2)
            for s in range(16):
                i = tr(bank[7][:, s * NE:(s + 1) * NE], bgu[:, s * P:(s + 1) * P], ident[0:NE, 0:NE])
            i.then_inc(S("bias_T"), 1)
            pe.wait_ge(S("h2_ready"), TT)
            for n in range(4):
                for k in (2 * n, 2 * n + 1):
                    for t in range(TT):
                        i = tr(bank[2 + n][:, (k % 2) * T + t * P:(k % 2) * T + (t + 1) * P],
                               h2[:, t, k * P:(k + 1) * P], ident[:, :])
                i.then_inc(S("h2_T"), 1)
            pe.wait_ge(S("h2T_ready"), 4)
            for t in range(TT):
                for k in range(KT):
                    i = mm(bank[6][:, t * NE:(t + 1) * NE], h2T[:, k, t * P:(t + 1) * P], wr[:, k, :],
                           start=(k == 0), stop=(k == KT - 1))
            i.then_inc(S("router_mm"), 1)
            pe.wait_ge(S("sel_ready"), 1)
            pe.wait_ge(S("late_consts"), 2)
            mm(bank[2][:, 0:NE], stri[:, :], sel[:, 0, :], start=True, stop=True)
            mm(bank[2][:, NE:2 * NE], ones[:, :], sel[:, 0, :], start=True, stop=False)
            mm(bank[2][:, NE:2 * NE], stri[:, :], sel[:, 1, :], start=False, stop=True)
            mm(bank[2][:, 2 * NE:3 * NE], ones[:, :], sel[:, 0, :], start=True, stop=False)
            mm(bank[2][:, 2 * NE:3 * NE], ones[:, :], sel[:, 1, :], start=False, stop=True)\
                .then_inc(S("rank_mm"), 1)
            for t in range(TT):
                i = tr(bank[3][0:NE, t * P:(t + 1) * P], gates[:, t, :], ident[:, :])
            i.then_inc(S("gT_mm"), 1)
            pe.wait_ge(S("gT_ready"), 1)
            pe.wait_ge(S("biasT_ready"), 1)
            for t in range(TT):
                for half in range(NOUT):
                    i = mm(bank[4 + 2 * t + half][:, :], gT[:, t * P:(t + 1) * P], bdn[:, half * NC:(half + 1) * NC],
                           start=True, stop=False)
            i.then_inc(S("init_mm"), 1)

            def gather(i, half):
                pe.wait_ge(S("onehot_ready"), i + 1)
                if not isinstance(i, int):
                    pe.wait_ge(*((S("scat_ready"), i) if half == 0 else (S("xg_ready"), 2 * i + 1)))
                elif half == 0 and i:
                    pe.wait_ge(S("scat_ready"), i)
                elif half == 1:
                    pe.wait_ge(S("xg_ready"), 2 * i + 1)
                for n in range(2 * TT):
                    t, part = n // 2, (h_hi, h_lo)[n % 2]
                    g = mm(bank[3][:, :], onehot[:, t, :, :].rearrange("p a c -> p (a c)"),
                           part[:, t, half * NC:(half + 1) * NC], start=(n == 0), stop=(n == 2 * TT - 1))
                g.then_inc(S("xg_mm"), 1)

            def turn_tokens(i):
                pe.wait_ge(S("xg_ready"), 2 * i + 2)
                for k in range(KT):
                    g = mm(bank[3][:, k * CAP:(k + 1) * CAP], xg[0:CAP, k * P:(k + 1) * P],
                           ident[0:CAP, 0:CAP], is_transpose=k > 0, start=True, stop=True)
                g.then_inc(S("xT_mm"), 1)

            def turn_gates(i):
                pe.wait_ge(S("xT_ready"), i + 1)
                for t in range(TT):
                    g = tr(bank[3][:, t * P:(t + 1) * P], gatehot[:, t, :, :].rearrange("p a c -> p (a c)"),
                           ident[:, :])
                g.then_inc(S("st_mm"), 1)

            def multiply(i, cc, h):
                q = EC * i + cc
                looped = not isinstance(i, int)
                if h == 0:
                    if cc == 0:
                        pe.wait_ge(S("xT_ready"), i + 1)
                        if looped:
                            pe.wait_ge(S("tr_ev"), 4 * i)
                    elif cc in (1, 2):
                        if looped:
                            pe.wait_ge(S("acc_ev"), EC * i - 2 + cc)
                    elif cc == 3:
                        pe.wait_ge(S("tr_ev"), 4 * i + 1)
                    elif cc == 4:
                        pe.wait_ge(S("tr_ev"), 4 * i + 3)
                        pe.wait_ge(S("aT_ready"), 2 * i + 1)
                    else:
                        pe.wait_ge(S("aT_ready"), 2 * i + 2)
                pe.wait_ge(S("lo_ready"), 2 * q + h + 1)
                for j in range(4 * h, 4 * h + 4):
                    for w in (w_hi, w_lo):
                        if cc < 4:
                            o, src, k = bank[ACC[cc]], xT, j
                            start, stop = j == 0 and w is w_hi, j == KT - 1 and w is w_lo
                        else:
                            o, src, k = bank[ACC[4 + j % 2]], aT, 4 * (cc - 4) + j // 2
                            start, stop = k == 0 and w is w_hi, k == KT - 1 and w is w_lo
                        g = mm(o[:, :], src[:, k, :, :].rearrange("p a c -> p (a c)"), w[:, cc % 2, j, :],
                               start=start, stop=stop)
                g.then_inc(S("half_mm"), 1)

            def turn(i, cc):
                pe.wait_ge(S("acc_ev"), EC * i + cc + 1)
                for s in range(4):
                    g = tr(bank[ACC[cc]][:, s * P:(s + 1) * P], evac[:, cc % 3, s * P:(s + 1) * P], ident[:, :])
                g.then_inc(S("turned"), 1)

            def scatter(i, half, last_=False):
                pe.wait_ge(S("acc_ev"), EC * i + half + 5)
                pe.wait_ge(S("scat_ready"), i + 1)
                for t in range(TT):
                    g = mm(bank[4 + 2 * t + half][:, :], scat[:, t * P:(t + 1) * P], evac[:, (4 + half) % 3, :],
                           start=False, stop=last_)
                g.then_inc(S("scattered"), 1)

            def item(i, first):
                multiply(i, 0, 0)
                if not first:
                    scatter(i - 1, 0)
                multiply(i, 0, 1)
                multiply(i, 1, 0)
                turn(i, 0)
                multiply(i, 1, 1)
                if not first:
                    scatter(i - 1, 1)
                turn_gates(i)
                multiply(i, 2, 0)
                turn(i, 1)
                multiply(i, 2, 1)
                multiply(i, 3, 0)
                turn(i, 2)
                multiply(i, 3, 1)
                gather(i + 1, 0)
                multiply(i, 4, 0)
                turn(i, 3)
                multiply(i, 4, 1)
                gather(i + 1, 1)
                turn_tokens(i + 1)
                multiply(i, 5, 0)
                multiply(i, 5, 1)

            pe.wait_ge(S("items_ready"), 2)
            n_it = pe.value_load(n_items[0:1, 0:1], min_val=0, max_val=NI - NE) + NE
            pe.wait_ge(S("hlo_ready"), TT)
            gather(0, 0)
            gather(0, 1)
            turn_tokens(0)
            item(0, True)
            with pe.Fori(1, n_it) as i:
                item(i, False)
            scatter(n_it - 1, 0, True)
            scatter(n_it - 1, 1, True)


NROWDMA = 16


def kernel(**inputs):
    import numpy as np
    import concourse.bacc as bacc
    from concourse.bass_utils import run_bass_kernel_spmd

    nc = bacc.Bacc("TRN2", target_bir_lowering=False, num_devices=1)
    arrays, args = {}, []
    for name in _INS:
        a = np.ascontiguousarray(inputs[name])
        arrays[f"in_{name}"] = a
        args.append(nc.dram_tensor(f"in_{name}", a.shape, mybir.dt.from_np(a.dtype), kind="ExternalInput").ap())
    args.append(nc.dram_tensor("out", (1, T, D), F32, kind="ExternalOutput").ap())
    build(nc, *args)
    r = run_bass_kernel_spmd(nc, [arrays], core_ids=[0])
    return r.results[0]["out"]


_INS = ['x', 'c', 'w_ada', 'b_ada', 'norm1_g', 'w_in', 'mu_shift', 'w0', 'w2', 'a0', 'a2', 'g2', 'k_k', 'k_a',
        'r_k', 'gn_w', 'gn_b', 'b_f', 'q_norm_g', 'k_norm_g', 'o_norm_g', 'w_out', 'norm2_g', 'w_router',
        'b_router', 'w_gate_up', 'b_gate_up', 'w_down', 'b_down', 'final_g']
```

```python
import concourse.bass as bass
from concourse import mybir
from contextlib import ExitStack

F32 = mybir.dt.float32
F32R = mybir.dt.float32r
I32 = mybir.dt.int32
I8 = mybir.dt.int8
U32 = mybir.dt.uint32
ALU = mybir.AluOpType
ACT = mybir.ActivationFunctionType
AX = mybir.AxisListType

P = 128
D = 1024
KT = D // P
T = 256
TT = T // P
HD = 64
NH = 8
NF = NH * HD // P
NC = 512
RT = 14
INT = 31
NU = NH * TT
NE = 32
TOPK = 4
CAP = 64
NI = NE + T * TOPK // CAP
RING = 6
NADA = 6 * D // NC
NROWS = NADA - 4
NIN = 8
NOUT = D // NC
EC = 6
LEVELS = (1, 2, 4, 8, 16, 32, 64)
STEPS = 4 * (len(LEVELS) - 1)
NORM_EPS = 1e-6
GN_EPS = 64e-5
EXPM05 = 0.6065306597126334
ALPHA = 1.702
LIMIT = 7.0

ROWS = [('c', 8), ('norm1_g', 8), ('mu_shift', 14), ('w0', 4), ('a0', 4), ('k_k', 4), ('k_a', 4),
        ('r_k', 4), ('gn_w', 4), ('gn_b', 4), ('q_norm_g', 1), ('k_norm_g', 1), ('o_norm_g', 1),
        ('b_ada', 16)]
ROW = {}
for _name, _n in ROWS:
    ROW[_name] = sum(n for m, n in ROWS[:len(ROW)])
NROW = sum(n for _, n in ROWS)


def build(nc, x, c, w_ada, b_ada, norm1_g, w_in, mu_shift, w0, w2, a0, a2, g2, k_k, k_a, r_k, gn_w,
          gn_b, b_f, q_norm_g, k_norm_g, o_norm_g, w_out, norm2_g, w_router, b_router, w_gate_up,
          b_gate_up, w_down, b_down, final_g, out, dbg=None):
    ctx = ExitStack()
    with ctx:
        sems = {}

        def S(name):
            if name not in sems:
                sems[name] = ctx.enter_context(nc.semaphore(name))
            return sems[name]

        def place(name, shape, dt, offset):
            n = 1 if dt == I8 else 4
            for d in shape[1:]:
                n *= d
            assert offset + n <= nc.sbuf_usable_end, (name, offset + n - nc.sbuf_usable_end)
            return nc.alloc_sbuf_tensor_at(name, list(shape), dt, offset=offset), offset + (n + 31) // 32 * 32

        class Region:

            def __init__(self, offset):
                self.at = offset

            def __call__(self, name, shape, dt=F32):
                t, self.at = place(name, shape, dt, self.at)
                return t

        both = Region((nc.sbuf_base + 63) // 64 * 64)
        raw = both("raw", [P, RING, KT, NC])
        ident = both("ident", [P, P])
        items = both("items", [1, NI + 2], I32)
        n_items = both("n_items", [1, 2], I32)
        last_item = both("last_item", [1, NE], I32)
        pos = both("pos", [P, TT, NE])
        gates = both("gates", [P, TT, NE])
        slots = both("slots", [P, 2, CAP])
        base = both.at

        moe = Region(base)
        w_hi = moe("w_hi", [P, 2, KT, NC], F32R)
        w_lo = moe("w_lo", [P, 2, KT, NC], F32R)
        h_hi = moe("h_hi", [P, TT, D], F32R)
        h_lo = moe("h_lo", [P, TT, D], F32R)
        xT = moe("xT", [P, KT, 2, CAP], F32R)
        aT = moe("aT", [P, KT, 2, CAP], F32R)
        xg = moe("xg", [P, D])
        evac = moe("evac", [P, 3, NC])
        biasT = moe("biasT", [P, NE, 4, 4])
        bias_i = moe("bias_i", [P, 4, 4])
        onehot = moe("onehot", [P, TT, 2, CAP], F32R)
        gatehot = moe("gatehot", [P, TT, 2, CAP])
        scat = moe("scat", [P, T])
        gated = moe("gated", [P, 2, 4, CAP])
        sig = moe("sig", [P, 2, 4, CAP])
        ups = moe("ups", [P, 2, 4, CAP])

        SLOT = 4096

        def at_slot(n, name, shape, dt=F32, off=0):
            return place(name, shape, dt, base + n * SLOT + off)[0]

        pz = at_slot(0, "pz", [P, RT, T + 1])
        AR = at_slot(0, "AR", [P, NF, TT, 2, P])
        Kr = at_slot(2, "Kr", [P, NF, TT, P])
        nBr = at_slot(3, "nBr", [P, NF, TT, P])
        x_sb = at_slot(4, "x_sb", [P, TT, D])
        r_f = at_slot(4, "r_f", [P, NF, T])
        k_f = at_slot(5, "k_f", [P, NF, T])
        v_f = at_slot(6, "v_f", [P, NF, T])
        logd = at_slot(7, "logd", [P, NF, T])
        a_f = at_slot(8, "a_f", [P, NF, T])
        kk_f = at_slot(9, "kk_f", [P, NF, T])
        b_f_ = at_slot(10, "b_f_", [P, NF, T])
        cum = at_slot(11, "cum", [P, NF, T])
        LR = at_slot(4, "LR", [P, NU, 4, P])
        pf = at_slot(12, "pf", [P, 16, T])
        T_CHUNK = 3
        ring_slot = (4 + 2 * NIN + NOUT + T_CHUNK) % RING
        ring_at = (nc.sbuf_base + 63) // 64 * 64 + ring_slot * KT * NC * 4
        Ti = place("Ti", [P, NU, P], F32, ring_at)[0]
        TiT = place("TiT", [P, NU, P], F32, ring_at + NU * P * 4)[0]
        lora = at_slot(16, "lora", [P, 2, T])
        loraa = at_slot(16, "loraa", [P, 2, T], off=2048)
        e_a = at_slot(16, "e_a", [P, NF, T])
        fvt = at_slot(16, "fvt", [P, TT, NH * HD])
        XT_ = at_slot(3, "XT_", [P, 2, 4, P])
        dtmp = at_slot(17, "dtmp", [P, NF, T])
        pr = at_slot(17, "pr", [P, 2, 3 * P])
        mix_r = at_slot(17, "mix_r", [P, NF, T])
        e_b = at_slot(18, "e_b", [P, NF, T])
        mix_f = at_slot(18, "mix_f", [P, NF, T])
        g_f = at_slot(19, "g_f", [P, NF, T])
        lora_w = at_slot(20, "lora_w", [P, NC])
        g2_sb = at_slot(20, "g2_sb", [P, NC], off=2048)
        bonus = at_slot(20, "bonus", [P, NF, T])
        acc = at_slot(21, "acc", [P, 2, NC])
        R0 = at_slot(21, "R0", [P, NF, P])
        nBbt = at_slot(21, "nBbt", [P, NC], off=2048)
        hT = at_slot(22, "hT", [P, KT, T])
        Vt = at_slot(22, "Vt", [P, TT, NC])
        A0t = at_slot(23, "A0t", [P, NC])
        Kbt = at_slot(23, "Kbt", [P, NC], off=2048)
        brows = at_slot(24, "brows", [NROWS, NC])
        A0 = at_slot(24, "A0", [P, NF, P])
        Kb = at_slot(24, "Kb", [P, NF, P], off=2048)
        nBb = at_slot(17, "nBb", [P, NF, P], off=2048)
        fsq = at_slot(24, "fsq", [P, NF, T])
        prT = at_slot(24, "prT", [P, 2, 3 * P])
        tail = Region(base + 25 * SLOT)
        ones = tail("ones", [P, P])
        blk = tail("blk", [P, P])
        lrmask = tail("lrmask", [P, 2, P], I32)
        lev = tail("lev", [P, len(LEVELS), P], I8)
        levT = tail("levT", [P, len(LEVELS), P], I8)
        causal = tail("causal", [P, P])
        colv = tail("colv", [P, NROW])
        fz = tail("fz", [NH, T])
        ncum = tail("ncum", [NH, T])
        mrows = tail("mrows", [NROWS, NC])
        pick = tail("pick", [P, 2 * NROWS])
        rowv = at_slot(16, "rowv", [NROW, P])
        xsq = at_slot(8, "xsq", [P, TT, D])
        csil = tail("csil", [P, KT])
        modc = tail("modc", [P, 16])
        ss = tail("ss", [P, 2])
        rs = tail("rs", [P, 2])
        bfc = tail("bfc", [NH, 1])
        nmid = tail("nmid", [P, NF, TT])
        rmax = tail("rmax", [P, 2, 2])
        rsum = tail("rsum", [P, 2, 2])
        rinv = tail("rinv", [P, 2, 2])
        TMV = at_slot(0, "TMV", [P, TT, NC])
        TA = at_slot(2, "TA", [P, NC], off=2048)
        MV = at_slot(1, "MV", [P, TT, NC])
        QT = at_slot(2, "QT", [P, NF, P])
        Z1 = at_slot(3, "Z1", [P, NF, HD])
        ysq = at_slot(22, "ysq", [P, NF, T])
        yrs = at_slot(23, "yrs", [P, NF, T])
        yT = at_slot(21, "yT", [P, NF, T])
        x1 = at_slot(4, "x1", [P, TT, D])
        gate1 = at_slot(6, "gate1", [P, D])
        shift2 = at_slot(7, "shift2", [P, D])
        scale2 = at_slot(8, "scale2", [P, D])
        n2g = at_slot(9, "n2g", [P, D])
        h2 = at_slot(10, "h2", [P, TT, D])
        h2T = at_slot(12, "h2T", [P, KT, T])
        bgu = at_slot(14, "bgu", [NE, 2 * D])
        wr = at_slot(0, "wr", [P, KT, NE])
        bdn = at_slot(1, "bdn", [NE, D])
        rt = Region(base + 2 * SLOT)
        brt = rt("brt", [P, NE])
        logits = rt("logits", [P, TT, NE])
        top8 = rt("top8", [P, TT, 8])
        idx8 = rt("idx8", [P, TT, 8], U32)
        idxf = rt("idxf", [P, TT, 8])
        texp = rt("texp", [P, TT, TOPK])
        tsum = rt("tsum", [P, TT])
        gk = rt("gk", [P, TT, TOPK, NE])
        sel = rt("sel", [P, TT, NE])
        cnt = rt("cnt", [P, NE])
        ge = rt("ge", [P, 4, NE])
        nblk = rt("nblk", [P, NE])
        binc = rt("binc", [P, NE])
        bexc = rt("bexc", [P, NE])
        gT = rt("gT", [NE, T])
        stri = rt("stri", [P, P])
        iota_e = rt("iota_e", [P, NE])
        iota_i = rt("iota_i", [1, NI + 2])
        icmp = at_slot(20, "icmp", [1, NI + 2, NE])
        isum = rt("isum", [1, NI + 2])
        ss2 = rt("ss2", [P, 2])
        rs2 = rt("rs2", [P, 2])
        assert rt.at <= base + 4 * SLOT
        x1q = at_slot(22, "x1q", [P, D])
        yo = at_slot(4, "yo", [P, TT, D])
        yq = at_slot(6, "yq", [P, D])
        ss3 = at_slot(7, "ss3", [P, 2])
        rs3 = at_slot(7, "rs3", [P, 2], off=64)

        mod_d = nc.dram_tensor("mod_rows", [4 * D], F32, kind="Internal").ap()
        x1_d = nc.dram_tensor("x1_rows", [T, D], F32, kind="Internal").ap()

        bank = [ctx.enter_context(nc.psum_tensor(f"bank{i}", [P, NC], F32)) for i in range(8)]

        def wview(w):
            return w.rearrange("(k p) n -> p k n", p=P)

        stream = [('ada', j) for j in range(4)]
        for j in range(NIN):
            stream += [('in', j), ('ada', 4 + j)]
        stream += [('out', j) for j in range(NOUT)]
        NS = len(stream)
        where = {u: n for n, u in enumerate(stream)}

        def slot_of(n):
            return n % RING

        def loaded(n):
            return S(f"w_loaded{n % RING}"), 16 * (n // RING + 1)

        def used(n):
            kind, j = stream[n]
            return {'ada': (S("ada_used"), j + 1), 'in': (S("p_mm"), min(4 * j + 4, INT)),
                    'out': (S("wo_mm"), TT * (j + 1))}[kind]

        def item_slot(cc):
            return (NS + cc) % RING

        def item_loaded(cc):
            return S(f"w_loaded{item_slot(cc)}"), 16 * ((NS + cc) // RING + 1)


        POOL_LO = [(1, 1), (5, 1)]
        DVE_LO = [(cc, h) for cc in range(EC) for h in range(2) if (cc, h) not in POOL_LO]

        def lo_done(i, cc, h):
            mine, name = (POOL_LO, "pool_lo") if (cc, h) in POOL_LO else (DVE_LO, "dve_lo")
            return S(name), i * len(mine) + mine.index((cc, h)) + 1

        def slot_free(i, cc):
            if (cc, 0) in POOL_LO or (cc, 1) in POOL_LO:
                return S("half_mm"), 2 * (EC * i + cc) + 2
            return lo_done(i, cc, 1)

        ACC = (2, 0, 1, 2, 0, 1)
        GU_COLS = [0, D, NC, D + NC]
        gu_view = w_gate_up[0].rearrange("e (k p) n -> e p k n", p=P)
        dn_view = w_down[0].rearrange("e (k p) n -> e p k n", p=P)

        def chunk_src(e, cc):
            if cc < 4:
                at0 = GU_COLS[cc]
                return gu_view[bass.ds(e, 1), :, :, at0:at0 + NC].rearrange("e p k n -> (e p) k n")
            return dn_view[bass.ds(e, 1), :, 4 * (cc - 4):4 * (cc - 3), :].rearrange("e p k n -> (e p) k n")

        def chunk_dst(cc):
            dst = raw[:, item_slot(cc), :, :]
            return dst if cc < 4 else dst.rearrange("p (k h) n -> p k (h n)", h=2)

        last = raw[:, item_slot(0), :, :].rearrange("p k n -> p (k n)")
        x1e, gate2, fg = last[:, 0:2 * D], last[:, 2 * D:3 * D], last[:, 3 * D:4 * D]

        def tile_of(h):
            return h // 2, slice(HD * (h % 2), HD * (h % 2) + HD)

        def colof(name, i=0, n=1):
            return colv[:, ROW[name] + i:ROW[name] + i + n]

        block = ctx.enter_context(nc.Block())

        @block.sync
        def _(sp):
            sp.dma_start(x_sb[:, :, :], x[0].rearrange("(t p) n -> p t n", p=P)).then_inc(S("x_in"), 16)
            for n, (kind, j) in enumerate(stream):
                if n >= RING:
                    sp.wait_ge(*used(n - RING))
                if n == 1:
                    sp.wait_ge(S("rows_in"), 16 * NROWDMA)
                    sp.wait_ge(S("lora_in"), 16 * 3)
                src = {'ada': w_ada, 'in': w_in, 'out': w_out}[kind][0]
                w = min(NC, src.shape[1] - j * NC)
                sp.dma_start(raw[:, n % RING, :, 0:w], wview(src)[:, :, j * NC:j * NC + w])\
                  .then_inc(S(f"w_loaded{n % RING}"), 16)
            for cc in range(EC):
                sp.wait_ge(*used(NS + cc - RING))
                if cc == T_CHUNK:
                    sp.wait_ge(S("tx_mm"), 3)
                sp.dma_start(chunk_dst(cc), chunk_src(0, cc))\
                  .then_inc(S(f"w_loaded{item_slot(cc)}"), 16)
            sp.wait_ge(S("items_ready"), 3)
            n_it = sp.value_load(n_items[0:1, 0:1], min_val=0, max_val=NI - NE) + NE
            with sp.Fori(1, NE) as e:
                before = sp.value_load(last_item[0:1, bass.ds(e - 1, 1)], min_val=0, max_val=NI)
                for cc in range(EC):
                    sp.wait_ge(*slot_free(before, cc))
                    sp.dma_start(chunk_dst(cc), chunk_src(e, cc))\
                      .then_inc(S(f"w_loaded{item_slot(cc)}"), 16)
            sp.wait_ge(*slot_free(n_it - 1, 0))
            sp.wait_ge(S("x1_out"), 16)
            sp.dma_start(x1e.rearrange("p (t n) -> p t n", t=TT), x1_d.rearrange("(t p) n -> p t n", p=P))\
              .then_inc(S("end_in"), 16)
            sp.dma_start(gate2, mod_d[3 * D:4 * D].partition_broadcast(P)).then_inc(S("end_in"), 16)
            sp.dma_start(fg, final_g.partition_broadcast(P)).then_inc(S("end_in"), 16)
            sp.wait_ge(S("out_ready"), TT)
            sp.dma_start(out[0].rearrange("(t p) n -> p t n", p=P), yo[:, :, :]).then_inc(S("out_done"), 16)
            sp.wait_ge(S("out_done"), 16)

        @block.gpsimd
        def _(pool):
            made = [0]

            def step(ins):
                made[0] += 1
                ins.then_inc(S("pool_step"), 1)
                pool.wait_ge(S("pool_step"), made[0])

            g = nc.gpsimd

            def keep(t, pattern, base_, mult, op=ALU.is_ge, fill=0.0):
                step(g.affine_select(out=t, in_=t, compare_op=op, fill=fill, base=base_,
                                     pattern=pattern, channel_multiplier=mult))

            step(g.memset(ident[:, :], 0.0))
            keep(ident[:, :], [[-1, P]], 0, 1, ALU.not_equal, 1.0)
            step(g.memset(pick[:, :], 0.0))
            step(g.memset(pick[:, NROWS:NROWS + 1], 1.0))
            g.memset(ones[:, :], 1.0).then_inc(S("consts"), 1)
            step(g.memset(blk[:, :], 1.0))
            keep(blk[:, HD:P], [[0, HD]], -HD, 1)
            keep(blk[:, 0:HD], [[0, HD]], HD - 1, -1)
            step(g.memset(lrmask[:, :, :], 1))
            keep(lrmask[:, 0, :], [[1, P]], -1, -1)
            keep(lrmask[:, 1, :], [[1, P]], 0, -1)
            step(g.memset(causal[:, :], 0.0))
            keep(causal[:, :], [[-1, P]], 0, 1, ALU.is_ge, -1e30)
            step(g.memset(lev[:, :, :], 0))
            step(g.memset(levT[:, :, :], 0))
            for n, m in enumerate(LEVELS):
                nb = P // (2 * m)
                for t, half, lo_, hi_ in ((lev, 0, m, 2 * m - 1), (levT, 1, 0, m - 1)):
                    v = t[:, n, :].rearrange("p (b w) -> p b w", w=2 * m)[:, :, half * m:half * m + m]
                    step(g.memset(v, 1))
                    keep(v, [[-2 * m, nb], [0, m]], -lo_, 1)
                    keep(v, [[2 * m, nb], [0, m]], hi_, -1)
            g.iota(slots[:, :, :], pattern=[[0, 2], [1, CAP]], base=0, channel_multiplier=0,
                   allow_small_or_imprecise_dtypes=True).then_inc(S("consts"), 1)
            pool.wait_ge(S("ew_done"), 1)
            pool.wait_ge(S("tm_T"), 2)
            g.memset(LR[:, :, :, :], 0.0).then_inc(S("LR_zero"), 1)
            pool.wait_ge(*used(NS + T_CHUNK - RING))
            for t in (Ti, TiT):
                g.tensor_copy(t[:, :, :], ident[:, :].unsqueeze(1).to_broadcast([P, NU, P]))\
                 .then_inc(S("T_ident"), 1)
            pool.wait_ge(S("y_mm"), 3)
            pool.wait_ge(S("mixf_ready"), 1)
            pool.wait_ge(S("mod_out"), 16)
            pool.dma_start(x1[:, :, :], x[0].rearrange("(t p) n -> p t n", p=P)).then_inc(S("late_in"), 16)
            for n, t in enumerate((gate1, shift2, scale2)):
                pool.dma_start(t[:, :], mod_d[n * D:(n + 1) * D].partition_broadcast(P))\
                    .then_inc(S("late_in"), 16)
            pool.dma_start(n2g[:, :], norm2_g[0].partition_broadcast(P)).then_inc(S("late_in"), 16)
            pool.dma_start(wr[:, :, :], wview(w_router[0])).then_inc(S("late2_in"), 16)
            pool.dma_start(bdn[:, :], b_down[0]).then_inc(S("late2_in"), 16)
            pool.dma_start(bgu[:, :], b_gate_up[0]).then_inc(S("late2_in"), 16)
            pool.dma_start(brt[:, :], b_router[0].partition_broadcast(P)).then_inc(S("late2_in"), 16)
            step(g.memset(stri[:, :], 1.0))
            keep(stri[:, :], [[1, P]], -1, -1)
            g.iota(iota_e[:, :], pattern=[[1, NE]], base=0, channel_multiplier=0,
                   allow_small_or_imprecise_dtypes=True).then_inc(S("late_consts"), 1)
            g.iota(iota_i[:, :], pattern=[[1, NI + 2]], base=0, channel_multiplier=0,
                   allow_small_or_imprecise_dtypes=True).then_inc(S("late_consts"), 1)
            pool.wait_ge(S("x1_ready"), 4)
            pool.dma_start(x1_d.rearrange("(t p) n -> p t n", p=P), x1[:, :, :]).then_inc(S("x1_out"), 16)
            pool.wait_ge(S("x1_out"), 16)

            def select(i):
                e_i = pool.value_load(items[0:1, bass.ds(i, 1)], min_val=0, max_val=NE - 1)

                pool.wait_ge(S("onehot_ready"), i + 1)
                for t in range(TT):
                    ins = g.tensor_tensor(gatehot[:, t, :, :], onehot[:, t, :, :].bitcast(F32),
                                          gates[:, t, bass.ds(e_i, 1)].unsqueeze(2).to_broadcast([P, 2, CAP]),
                                          ALU.mult)
                ins.then_inc(S("gatehot_ready"), 1)

            def lo(i, cc, h):
                pool.wait_ge(S("hi_ready"), 2 * (EC * i + cc) + h + 1)
                part = slice(4 * h, 4 * h + 4)
                g.tensor_tensor(w_lo[:, cc % 2, part, :], raw[:, item_slot(cc), part, :],
                                w_hi[:, cc % 2, part, :].bitcast(F32), ALU.subtract).then_inc(S("pool_lo"), 1)

            def weigh(i):
                pool.wait_ge(S("st_mm"), i + 1)
                select(i + 1)

            def item(i):
                lo(i, 1, 1)
                lo(i, 5, 1)
                weigh(i)

            pool.wait_ge(S("items_ready"), 3)
            n_it = pool.value_load(n_items[0:1, 0:1], min_val=0, max_val=NI - NE) + NE
            pool.wait_ge(S("moe_free"), 1)
            select(0)
            item(0)
            with pool.Fori(1, n_it) as i:
                item(i)

        @block.scalar
        def _(act_e):
            a = nc.scalar
            nrows = 0
            for name, src in (('c', c[0]), ('norm1_g', norm1_g[0]), ('mu_shift', mu_shift[0]), ('w0', w0[0]),
                              ('a0', a0[0]), ('k_k', k_k[0]), ('k_a', k_a[0]), ('gn_w', gn_w[0]),
                              ('gn_b', gn_b[0]), ('b_ada', b_ada[0, 0:2 * D])):
                n = src.shape[0] // P
                act_e.dma_start(rowv[ROW[name]:ROW[name] + n, :], src.rearrange("(r n) -> r n", n=P))\
                     .then_inc(S("rows_in"), 16)
                nrows += 1
            act_e.dma_start(rowv[ROW['r_k']:ROW['r_k'] + 4, :], r_k[0].rearrange("(r h) n -> r (h n)", h=2))\
                 .then_inc(S("rows_in"), 16)
            nrows += 1
            for name, src in (('q_norm_g', q_norm_g), ('k_norm_g', k_norm_g), ('o_norm_g', o_norm_g)):
                for half in range(2):
                    act_e.dma_start(rowv[ROW[name]:ROW[name] + 1, HD * half:HD * half + HD], src)\
                         .then_inc(S("rows_in"), 16)
                    nrows += 1
            assert nrows == NROWDMA
            act_e.dma_start(lora_w[0:HD, :], w2[0]).then_inc(S("lora_in"), 16)
            act_e.dma_start(lora_w[HD:P, :], a2[0]).then_inc(S("lora_in"), 16)
            act_e.dma_start(g2_sb[:, :], g2[0]).then_inc(S("lora_in"), 16)
            act_e.dma_start(brows[:, :], b_ada[0, 2 * D:].rearrange("(r n) -> r n", n=NC)).then_inc(S("brows_in"), 16)
            act_e.dma_start(bfc[:, :], b_f.rearrange("o h -> h o")).then_inc(S("bf_in"), 16)

            act_e.wait_ge(S("x_in"), 16)
            for t in range(TT):
                a.activation(xsq[:, t, :], x_sb[:, t, :], ACT.Square, accum_out=ss[:, t:t + 1])\
                 .then_inc(S("ss_ready"), 1)
            act_e.wait_ge(S("ms_ready"), 1)
            a.activation(rs[:, :], ss[:, :], ACT.Sqrt).then_inc(S("rms_ready"), 1)
            act_e.wait_ge(S("colv_ready"), 1)
            a.activation(csil[:, :], colof('c', 0, 8), ACT.Sigmoid).then_inc(S("csig"), 1)
            act_e.wait_ge(S("modc_ready"), 1)
            for k in range(KT):
                act_e.wait_ge(S("xnT"), k // 2 + 1)
                a.activation(hT[:, k, :], bank[k // 2][:, (k % 2) * T:(k % 2) * T + T], ACT.Identity,
                             bias=modc[:, k:k + 1], scale=modc[:, 8 + k:9 + k]).then_inc(S("hT_ready"), 1)

            def take_tile(m):
                act_e.wait_ge(S("p_mm"), m + 1)
                if m < RT:
                    i = a.activation(pz[:, m, 1:T + 1], bank[m % 4][:, 0:T], ACT.Copy)
                elif m < INT - 1:
                    i = a.activation(pf[:, m - RT, :], bank[m % 4][:, 0:T], ACT.Copy)
                else:
                    act_e.wait_ge(S("bf_in"), 16)
                    i = a.activation(fz[:, :], bank[m % 4][0:NH, 0:T], ACT.Identity, bias=bfc[:, 0:1])
                i.then_inc(S("p_ev"), 1)

            for m in range(15):
                take_tile(m)
            act_e.wait_ge(S("shifted"), 4)
            a.activation(loraa[0:HD, 0, :], lora[0:HD, 0, :], ACT.Tanh)
            a.activation(loraa[HD:P, 0, :], lora[HD:P, 0, :], ACT.Copy)
            a.activation(loraa[:, 1, :], lora[:, 1, :], ACT.Sigmoid).then_inc(S("lora_act"), 1)
            for q in range(6):
                act_e.wait_ge(S("lora_mm"), q + 1)
                for t in range(2):
                    m = 2 * (q % 2) + t
                    src = bank[5 + q % 3][:, t * T:(t + 1) * T]
                    if q < 2:
                        i = a.activation(logd[:, m, :], src, ACT.Sigmoid, bias=colof('w0', m))
                    elif q < 4:
                        i = a.activation(a_f[:, m, :], src, ACT.Sigmoid, bias=colof('a0', m))
                    else:
                        i = a.activation(g_f[:, m, :], src, ACT.Copy)
                i.then_inc(S("lora_ev"), 1)
            for m in range(15, 20):
                take_tile(m)
            for m in (20, 21):
                take_tile(m)
            for t in range(2):
                act_e.wait_ge(S("kksum_mm"), t + 1)
                a.activation(e_b[:, 2 * t:2 * t + 2, :], bank[5 + t][:, :].rearrange("p (m t) -> p m t", m=2),
                             ACT.Sqrt).then_inc(S("kknorm"), 1)
            take_tile(22)
            take_tile(23)
            for m in (24, 25):
                take_tile(m)
            act_e.wait_ge(S("d1_ready"), 1)
            a.activation(e_a[:, :, :], dtmp[:, :, :], ACT.Exp).then_inc(S("exps"), 1)
            a.activation(e_b[:, :, :], dtmp[:, :, :], ACT.Exp, scale=-1.0).then_inc(S("exps"), 1)
            take_tile(26)
            take_tile(27)
            act_e.wait_ge(S("d2_ready"), 1)
            a.activation(e_a[:, :, :], dtmp[:, :, :], ACT.Exp).then_inc(S("exps"), 1)
            take_tile(28)
            take_tile(29)
            take_tile(30)
            act_e.wait_ge(S("d3_ready"), 1)
            a.activation(e_b[:, :, 0:P], cum[:, :, P:T], ACT.Exp).then_inc(S("exps"), 1)
            a.activation(e_a[:, :, 0:P], e_a[:, :, P:T], ACT.Exp).then_inc(S("exps"), 1)
            act_e.wait_ge(S("d4_ready"), 1)
            a.activation(e_b[:, :, P:T], dtmp[:, 0:2, :].rearrange("p m (h t) -> p (m h) t", h=2), ACT.Exp,
                         scale=-1.0).then_inc(S("exps"), 1)
            act_e.wait_ge(S("fabs"), 1)
            a.activation(ncum[:, :], ncum[:, :], ACT.Exp).then_inc(S("fexp"), 1)
            act_e.wait_ge(S("fexp"), 1)
            a.activation(ncum[:, :], ncum[:, :], ACT.Ln, bias=1.0).then_inc(S("fln"), 1)
            act_e.wait_ge(S("acc_used"), NADA)
            a.activation(mrows[:, :], bank[4][0:NROWS, :], ACT.Copy).then_inc(S("mrows_ready"), 1)
            act_e.wait_ge(S("mrows_ready"), 1)
            act_e.dma_start(mod_d.rearrange("(r n) -> r n", n=NC), mrows[:, :]).then_inc(S("mod_out"), 16)
            for n, (dst, src) in enumerate(((Vt[:, 0, :], bank[5]), (Vt[:, 1, :], bank[6]), (A0t[:, :], bank[7]),
                                            (Kbt[:, :], bank[0]), (nBbt[:, :], bank[1]))):
                act_e.wait_ge(S("tm_T"), n + 1)
                a.activation(dst, src[:, :], ACT.Copy).then_inc(S("tm_ev"), 1)
            def take_prT(h):
                act_e.wait_ge(S("pr_T"), h + 1)
                if h >= 2:
                    act_e.wait_ge(S("o_mm"), h - 1)
                a.activation(prT[:, h % 2, :], bank[5][:, 0:3 * P], ACT.Copy).then_inc(S("prT_ready"), 1)

            for n in range(2):
                act_e.wait_ge(S("fms"), n + 1)
                a.activation(fsq[:, :, :], fsq[:, :, :], ACT.Sqrt).then_inc(S("frms"), 1)
            for t in range(TT):
                act_e.wait_ge(S("fv_T"), t + 1)
                a.activation(fvt[:, t, :], bank[5 + t][:, :], ACT.Copy).then_inc(S("fv_ev"), 1)
            for cc in range(TT):
                act_e.wait_ge(S("mv_mm"), cc + 1)
                a.activation(MV[:, cc, :], bank[cc][:, :], ACT.Copy).then_inc(S("mv_ev"), 1)
            act_e.wait_ge(S("qk_ready"), 2)
            for s in range(STEPS):
                act_e.wait_ge(S("x_mm"), s + 1)
                if s >= 2:
                    act_e.wait_ge(S("tt_mm"), s - 1)
                a.activation(XT_[:, s % 2, :, :], bank[(1, 4)[s % 2]][:, :].rearrange("p (u t) -> p u t", u=4),
                             ACT.Copy).then_inc(S("x_ev"), 1)
                if s % 3 == 1:
                    h = s // 3
                    act_e.wait_ge(S("smax"), h + 1)
                    for t in range(TT):
                        cols = slice(0, P) if t == 0 else slice(P, 3 * P)
                        i = a.activation(pr[:, h % 2, cols], pr[:, h % 2, cols], ACT.Exp,
                                         bias=rmax[:, h % 2, t:t + 1], accum_out=rsum[:, h % 2, t:t + 1])
                    i.then_inc(S("sexp"), 1)
                if s and s % 3 == 0:
                    take_prT(s // 3 - 1)
            take_prT(NH - 1)
            act_e.wait_ge(S("o_mm"), NH)
            for t in range(2):
                a.activation(fsq[:, 2 * t:2 * t + 2, :], bank[2 + t][:, :].rearrange("p (m t) -> p m t", m=2),
                             ACT.Square).then_inc(S("osq"), 1)
            for n, (dst, b) in enumerate(((TMV[:, 0, :], 1), (TMV[:, 1, :], 4), (TA[:, :], 6))):
                act_e.wait_ge(S("tx_mm"), n + 1)
                a.activation(dst, bank[b][:, :], ACT.Copy).then_inc(S("tx_ev"), 1)
            a.activation(pf[:, 12:16, :], pf[:, 12:16, :], ACT.Sigmoid).then_inc(S("ogate"), 1)
            act_e.wait_ge(S("z_mm"), 1)
            a.activation(Z1[:, :, :], bank[7][:, 0:T].rearrange("p (m v) -> p m v", m=NF), ACT.Copy)\
             .then_inc(S("z_ev"), 1)
            act_e.wait_ge(S("oms"), 1)
            a.activation(fsq[:, :, :], fsq[:, :, :], ACT.Sqrt).then_inc(S("orms"), 1)
            for t in range(2):
                act_e.wait_ge(S("y_mm"), 2 + t)
                a.activation(yT[:, 2 * t:2 * t + 2, :], bank[(1, 6)[t]][:, :].rearrange("p (m t) -> p m t", m=2),
                             ACT.Copy).then_inc(S("yT_ready"), 1)
            act_e.wait_ge(S("yc_ready"), 1)
            a.activation(ysq[:, :, :], yT[:, :, :], ACT.Square).then_inc(S("ysq_ready"), 1)
            act_e.wait_ge(S("yms"), 1)
            a.activation(yrs[:, :, :], yrs[:, :, :], ACT.Sqrt).then_inc(S("yrms"), 1)
            for t in range(TT):
                act_e.wait_ge(S("x1_ready"), 3 + t)
                if t:
                    act_e.wait_ge(S("ss_ready"), TT + t)
                a.activation(x1q[:, :], x1[:, t, :], ACT.Square, accum_out=ss2[:, t:t + 1])\
                 .then_inc(S("ss_ready"), 1)
            act_e.wait_ge(S("ms_ready"), 2)
            a.activation(rs2[:, :], ss2[:, :], ACT.Sqrt).then_inc(S("rms_ready"), 1)
            for t in range(TT):
                act_e.wait_ge(S("h2_ready"), t + 1)
                a.activation(h_hi[:, t, :], h2[:, t, :], ACT.Copy).then_inc(S("hhi_ready"), 1)
            for n in range(4):
                act_e.wait_ge(S("h2_T"), n + 1)
                a.activation(h2T[:, 2 * n:2 * n + 2, :], bank[2 + n][:, :].rearrange("p (k t) -> p k t", k=2),
                             ACT.Copy).then_inc(S("h2T_ready"), 1)
            act_e.wait_ge(S("tdiff"), 1)
            a.activation(texp[:, :, :], texp[:, :, :], ACT.Exp).then_inc(S("texp_ready"), 1)
            act_e.wait_ge(S("gT_mm"), 1)
            a.activation(gT[:, :], bank[3][0:NE, 0:T], ACT.Copy).then_inc(S("gT_ready"), 1)

            def hi(i, cc, h):
                q = EC * i + cc
                if h == 0:
                    act_e.wait_ge(S(f"w_loaded{item_slot(cc)}"), item_loaded(cc)[1] + 16 * expert[0])
                if not isinstance(i, int) or q >= 2:
                    act_e.wait_ge(S("half_mm"), 2 * q - 3 + h)
                a.activation(w_hi[:, cc % 2, 4 * h:4 * h + 4, :], raw[:, item_slot(cc), 4 * h:4 * h + 4, :],
                             ACT.Copy).then_inc(S("hi_ready"), 1)

            def take_acc(i, n):
                act_e.wait_ge(S("half_mm"), 2 * EC * i + 2 * min(n, 5) + 2 + 2 * (n == 4))
                looped = not isinstance(i, int)
                if n >= 3:
                    act_e.wait_ge(S("turned"), 4 * i + n - 2)
                elif n == 0 and looped:
                    act_e.wait_ge(S("turned"), 4 * i)
                elif looped:
                    act_e.wait_ge(S("scattered"), 2 * i - 2 + n)
                a.activation(evac[:, n % 3, :], bank[ACC[n]][:, :], ACT.Copy).then_inc(S("acc_ev"), 1)

            def take_xg(i, half):
                act_e.wait_ge(S("xg_mm"), 2 * i + half + 1)
                a.activation(xg[:, half * NC:(half + 1) * NC], bank[3][:, :], ACT.Copy).then_inc(S("xg_ready"), 1)

            def take_xT(i):
                act_e.wait_ge(S("xT_mm"), i + 1)
                a.activation(xT[:, :, 0, :], bank[3][:, :].rearrange("p (k c) -> p k c", k=KT), ACT.Copy)\
                 .then_inc(S("xThi_ready"), 1)

            def sigmoid(i, pair):
                act_e.wait_ge(S("gate_ready"), 2 * i + pair + 1)
                a.activation(sig[:, pair, :, :], gated[:, pair, :, :], ACT.Sigmoid, scale=ALPHA).then_inc(S("sig_ready"), 1)

            def act_hi(i, pair):
                act_e.wait_ge(S("act_ready"), 2 * i + pair + 1)
                a.activation(aT[:, 4 * pair:4 * pair + 4, 0, :], gated[:, pair, :, :], ACT.Copy)\
                 .then_inc(S("aThi_ready"), 1)

            def take_scat(i):
                act_e.wait_ge(S("st_mm"), i + 1)
                if not isinstance(i, int):
                    act_e.wait_ge(S("scattered"), 2 * i)
                a.activation(scat[:, :], bank[3][:, 0:T], ACT.Copy).then_inc(S("scat_ready"), 1)

            expert = [0]

            def item(i, first):
                if not first:
                    expert[0] = act_e.value_load(items[0:1, bass.ds(i, 1)], min_val=0, max_val=NE - 1)
                hi(i, 0, 0)
                take_xT(i)
                hi(i, 0, 1)
                hi(i, 1, 0)
                hi(i, 1, 1)
                if not first:
                    take_acc(i - 1, 4)
                hi(i, 2, 0)
                if not first:
                    take_acc(i - 1, 5)
                hi(i, 2, 1)
                take_acc(i, 0)
                hi(i, 3, 0)
                take_acc(i, 1)
                hi(i, 3, 1)
                hi(i, 4, 0)
                hi(i, 4, 1)
                take_acc(i, 2)
                sigmoid(i, 0)
                take_scat(i)
                hi(i, 5, 0)
                act_hi(i, 0)
                take_xg(i + 1, 0)
                take_acc(i, 3)
                hi(i, 5, 1)
                sigmoid(i, 1)
                take_xg(i + 1, 1)
                act_hi(i, 1)

            act_e.wait_ge(S("items_ready"), 3)
            n_it = act_e.value_load(n_items[0:1, 0:1], min_val=0, max_val=NI - NE) + NE
            act_e.wait_ge(S("moe_free"), 1)
            act_e.wait_ge(S("init_mm"), 1)
            act_e.wait_ge(S("x1_out"), 16)
            take_xg(0, 0)
            take_xg(0, 1)
            item(0, True)
            with act_e.Fori(1, n_it) as i:
                item(i, False)
            take_acc(n_it - 1, 4)
            take_acc(n_it - 1, 5)

            for t in range(TT):
                act_e.wait_ge(S("xo_ready"), t + 1)
                if t:
                    act_e.wait_ge(S("ss_ready"), 2 * TT + t)
                a.activation(yq[:, :], yo[:, t, :], ACT.Square, accum_out=ss3[:, t:t + 1])\
                 .then_inc(S("ss_ready"), 1)
            act_e.wait_ge(S("ms_ready"), 3)
            a.activation(rs3[:, :], ss3[:, :], ACT.Sqrt).then_inc(S("rms_ready"), 1)

        @block.vector
        def _(dve):
            v = nc.vector
            made = [0]

            def step(ins):
                made[0] += 1
                ins.then_inc(S("dve_step"), 1)
                dve.wait_ge(S("dve_step"), made[0])

            def ts(out_, in_, s1, s2, op0, op1=None):
                return v.tensor_scalar(out_, in_, s1, s2, op0, op1) if op1 is not None \
                    else v.tensor_scalar(out_, in_, s1, None, op0)

            def stt(out_, in0, s, in1, op0, op1):
                return v.scalar_tensor_tensor(out=out_, in0=in0, scalar=s, in1=in1, op0=op0, op1=op1)

            tt = v.tensor_tensor
            v.memset(pz[:, :, 0:1], 0.0)
            dve.wait_ge(S("rowsT"), 1)
            v.tensor_copy(colv[:, :], bank[5][:, 0:NROW]).then_inc(S("colv_ready"), 1)
            dve.wait_ge(S("colv_ready"), 1)
            step(ts(colof('q_norm_g'), colof('q_norm_g'), HD ** -0.5, None, ALU.mult))
            dve.wait_ge(S("ss_ready"), TT)
            ts(ss[:, :], ss[:, :], 1.0 / D, NORM_EPS, ALU.mult, ALU.add).then_inc(S("ms_ready"), 1)
            dve.wait_ge(S("rms_ready"), 1)
            step(v.reciprocal(rs[:, :], rs[:, :]))
            for t in range(TT):
                ts(x_sb[:, t, :], x_sb[:, t, :], rs[:, t:t + 1], None, ALU.mult).then_inc(S("xn_ready"), 1)
            dve.wait_ge(S("csig"), 1)
            step(tt(csil[:, :], csil[:, :], colof('c', 0, 8), ALU.mult))

            def ada(j):
                n = where[('ada', j)]
                dve.wait_ge(*loaded(n))
                if j >= 2:
                    dve.wait_ge(S("acc_used"), j - 1)
                o = acc[:, j % 2, :]
                for k in range(KT):
                    w = raw[:, slot_of(n), k, :]
                    i = stt(o, w, csil[:, k:k + 1], o, ALU.mult, ALU.add) if k \
                        else ts(o, w, csil[:, k:k + 1], None, ALU.mult)
                    if k < KT - 1:
                        step(i)
                    else:
                        i.then_inc(S("ada_used"), 1)

            for j in range(4):
                ada(j)
            dve.wait_ge(S("col_mm"), 1)
            step(tt(modc[:, :], bank[4][:, 0:16], colof('b_ada', 0, 16), ALU.add))
            stt(modc[:, 8:16], modc[:, 8:16], 1.0, colof('norm1_g', 0, 8), ALU.add, ALU.mult)\
                .then_inc(S("modc_ready"), 1)

            def shift(j):
                tiles = range(4 * j, min(4 * j + 4, RT))
                n = len(tiles)
                dve.wait_ge(S("p_ev"), tiles[-1] + 1)
                step(tt(dtmp[:, 0:n, :], pz[:, 4 * j:4 * j + n, 0:T], pz[:, 4 * j:4 * j + n, 1:T + 1],
                        ALU.subtract))
                dst = (r_f, k_f, v_f, lora)[j]
                for t, m in enumerate(tiles):
                    i = stt(dst[:, t, :], dtmp[:, t, :], colof('mu_shift', m), pz[:, m, 1:T + 1],
                            ALU.mult, ALU.add)
                i.then_inc(S("shifted"), 1)

            dve.wait_ge(S("consts"), 2)
            for j in range(4):
                ada(4 + j)
                shift(j)
            ada(8)
            dve.wait_ge(S("shifted"), 4)
            dve.wait_ge(S("lora_ev"), 6)
            step(ts(logd[:, :, :], logd[:, :, :], -EXPM05, None, ALU.mult))
            for m in range(NF):
                i = ts(kk_f[:, m, :], k_f[:, m, :], colof('k_k', m), None, ALU.mult)
            step(i)
            tt(dtmp[:, :, :], kk_f[:, :, :], kk_f[:, :, :], ALU.mult).then_inc(S("kksq_ready"), 1)
            ada(9)
            dve.wait_ge(S("kknorm"), 2)
            step(ts(e_b[:, :, :], e_b[:, :, :], 1e-12, None, ALU.max))
            step(v.reciprocal(e_b[:, :, :], e_b[:, :, :]))
            step(tt(kk_f[:, :, :], kk_f[:, :, :], e_b[:, :, :], ALU.mult))
            for m in range(NF):
                i = ts(dtmp[:, m, :], a_f[:, m, :], -1.0, colof('k_a', m), ALU.add, ALU.mult)
            step(i)
            step(stt(k_f[:, :, :], dtmp[:, :, :], 1.0, k_f[:, :, :], ALU.add, ALU.mult))
            tt(b_f_[:, :, :], kk_f[:, :, :], a_f[:, :, :], ALU.mult)
            for m in range(NF):
                i = stt(dtmp[:, m, :], r_f[:, m, :], colof('r_k', m), k_f[:, m, :], ALU.mult, ALU.mult)
            i.then_inc(S("rkk_ready"), 1)
            ada(10)
            for m in range(NF):
                for cc in range(TT):
                    i = v.tensor_tensor_scan(cum[:, m, cc * P:(cc + 1) * P],
                                             ones[:, 0:P], logd[:, m, cc * P:(cc + 1) * P], 0.0,
                                             ALU.mult, ALU.add)
            step(i)
            dve.wait_ge(S("bon_mm"), 2)
            for t in range(2):
                tt(bonus[:, 2 * t:2 * t + 2, :], bank[5 + t][:, :].rearrange("p (m t) -> p m t", m=2),
                   v_f[:, 2 * t:2 * t + 2, :], ALU.mult).then_inc(S("bon_ev"), 1)
            cumc = cum[:, :, :].rearrange("p m (c t) -> p (m c) t", c=TT)
            d1c = dtmp[:, :, :].rearrange("p m (c t) -> p (m c) t", c=TT)
            tt(d1c, cumc, cumc[:, :, HD - 1:HD].to_broadcast([P, NF * TT, P]), ALU.subtract)\
                .then_inc(S("d1_ready"), 1)
            r_c = r_f[:, :, :].rearrange("p m (c t) -> p m c t", c=TT)
            k_c, b_c, kk_c, e_ac, e_bc = (y[:, :, :].rearrange("p m (c t) -> p m c t", c=TT)
                                          for y in (k_f, b_f_, kk_f, e_a, e_b))
            dve.wait_ge(S("exps"), 2)
            tt(AR[:, :, :, 1, :], r_c, e_ac, ALU.mult)
            tt(Kr[:, :, :, :], k_c, e_bc, ALU.mult)
            stt(nBr[:, :, :, :].rearrange("p m c t -> p (m c t)"), b_f_[:, :, :].rearrange("p m t -> p (m t)"), -1.0,
                e_b[:, :, :].rearrange("p m t -> p (m t)"), ALU.mult, ALU.mult)
            dve.wait_ge(S("d1_ready"), 1)
            tt(dtmp[:, :, :], dtmp[:, :, :], logd[:, :, :], ALU.subtract).then_inc(S("d2_ready"), 1)
            ada(11)
            dve.wait_ge(S("exps"), 3)
            tt(AR[:, :, :, 0, :], kk_c, e_ac, ALU.mult).then_inc(S("A_ready"), 1)
            dve.wait_ge(S("A_ready"), 1)
            tt(e_a[:, :, P:T], cum[:, :, P:T], logd[:, :, P:T], ALU.subtract).then_inc(S("d3_ready"), 1)
            dlast = dtmp[:, 0:2, :].rearrange("p m (h t) -> p (m h) t", h=2)
            tt(dlast, cum[:, :, 0:P], cum[:, :, P - 1:P].to_broadcast([P, NF, P]), ALU.subtract)\
                .then_inc(S("d4_ready"), 1)
            dve.wait_ge(S("exps"), 5)
            dve.wait_ge(S("acc_used"), NADA)
            tt(R0[:, :, :], r_f[:, :, P:T], e_b[:, :, 0:P], ALU.mult)
            tt(A0[:, :, :], kk_f[:, :, P:T], e_a[:, :, 0:P], ALU.mult).then_inc(S("tm_src"), 1)
            dve.wait_ge(S("exps"), 6)
            tt(Kb[:, :, :], k_f[:, :, 0:P], e_b[:, :, P:T], ALU.mult).then_inc(S("tm_src"), 1)
            stt(nBb[:, :, :], b_f_[:, :, 0:P], -1.0, e_b[:, :, P:T], ALU.mult, ALU.mult)\
                .then_inc(S("tm_src"), 1)
            dve.wait_ge(S("p_ev"), INT)
            step(ts(ncum[:, :], fz[:, :], -1.0, None, ALU.mult))
            tt(ncum[:, :], ncum[:, :], fz[:, :], ALU.min).then_inc(S("fabs"), 1)
            dve.wait_ge(S("tm_src"), 3)
            dve.wait_ge(S("bon_ev"), 2)
            v.memset(rinv[:, :, :], 0.0).then_inc(S("ew_done"), 1)
            dve.wait_ge(S("fln"), 1)
            step(stt(fz[:, :], fz[:, :], 0.0, ncum[:, :], ALU.min, ALU.subtract))
            v.tensor_tensor_scan(ncum[:, :], ones[0:NH, 0:1].to_broadcast([NH, T]), fz[:, :], 0.0,
                                 ALU.mult, ALU.subtract).then_inc(S("ncum_ready"), 1)
            dve.wait_ge(S("tm_T"), 5)
            for n, name in enumerate(('q_norm_g', 'k_norm_g')):
                w = pf[:, 4 * n:4 * n + 4, :]
                tt(fsq[:, :, :], w, w, ALU.mult).then_inc(S("fsq_ready"), 1)
                dve.wait_ge(S("fsum_mm"), 2 * n + 2)
                for t in range(2):
                    i = ts(fsq[:, 2 * t:2 * t + 2, :], bank[2 + t][:, :].rearrange("p (m t) -> p m t", m=2),
                           1.0 / HD, NORM_EPS, ALU.mult, ALU.add)
                i.then_inc(S("fms"), 1)
                dve.wait_ge(S("frms"), n + 1)
                step(v.reciprocal(fsq[:, :, :], fsq[:, :, :]))
                i = stt(w, w, colof(name), fsq[:, :, :], ALU.mult, ALU.mult)
                i.then_inc(S("qk_ready"), 1)
                dve.wait_ge(S("qk_ready"), n + 1)
            dve.wait_ge(S("LR_zero"), 1)
            for u in range(NU):
                dve.wait_ge(S("lr_mm"), u + 1)
                b = bank[4 + u % 4][:, :].rearrange("p (a b t) -> p a (b t)", a=2, b=2)
                v.copy_predicated(LR[:, u, :, :].rearrange("p (a b) t -> p a (b t)", a=2),
                                  lrmask[:, :, :].rearrange("p b t -> p (b t)").unsqueeze(1).to_broadcast([P, 2, 2 * P]),
                                  b).then_inc(S("lr_ev"), 1)
            dve.wait_ge(S("T_ident"), 2)
            dve.wait_ge(S("lr_ev"), NU)
            for n, g in enumerate((2, 3, 0, 1)):
                dve.wait_ge(S("nL_T"), n + 1)
                us = slice(4 * g, 4 * g + 4)
                v.copy_predicated(Ti[:, us, :], lev[:, 0:1, :].to_broadcast([P, 4, P]),
                                  bank[g][:, :].rearrange("p (u t) -> p u t", u=4))
                v.copy_predicated(TiT[:, us, :], levT[:, 0:1, :].to_broadcast([P, 4, P]), LR[:, us, 0, :])\
                    .then_inc(S("T_up"), 1)

            def weigh(h):
                dve.wait_ge(S("s_mm"), h + 1)
                if h >= 2:
                    dve.wait_ge(S("pr_T"), h - 1)
                p_h = pr[:, h % 2, :]
                tt(p_h[:, 0:P], bank[0][:, 0:P], causal[:, :], ALU.add)
                tt(p_h[:, 2 * P:3 * P], bank[0][:, 2 * P:3 * P], causal[:, :], ALU.add)
                v.tensor_copy(p_h[:, P:2 * P], bank[0][:, P:2 * P]).then_inc(S("s_ev"), 1)
                dve.wait_ge(S("s_ev"), h + 1)
                v.tensor_reduce(rmax[:, h % 2, 0:1], p_h[:, 0:P], AX.X, ALU.max)
                step(v.tensor_reduce(rmax[:, h % 2, 1:2], p_h[:, P:3 * P], AX.X, ALU.max))
                ts(rmax[:, h % 2, :], rmax[:, h % 2, :], -1.0, None, ALU.mult).then_inc(S("smax"), 1)

            def normalize(h):
                p_h = pr[:, h % 2, :]
                dve.wait_ge(S("sexp"), h + 1)
                step(v.reciprocal(rinv[:, h % 2, :], rsum[:, h % 2, :]))
                ts(p_h[:, 0:P], p_h[:, 0:P], rinv[:, h % 2, 0:1], None, ALU.mult)
                ts(p_h[:, P:3 * P], p_h[:, P:3 * P], rinv[:, h % 2, 1:2], None, ALU.mult)\
                    .then_inc(S("pr_ready"), 1)

            for s in range(STEPS):
                n, g = 1 + s // 4, s % 4
                us = slice(4 * g, 4 * g + 4)
                dve.wait_ge(S("tt_mm"), s + 1)
                if n < len(LEVELS) - 1:
                    v.copy_predicated(Ti[:, us, :], lev[:, n:n + 1, :].to_broadcast([P, 4, P]),
                                      bank[6][:, :].rearrange("p (u t) -> p u t", u=4))
                v.copy_predicated(TiT[:, us, :], levT[:, n:n + 1, :].to_broadcast([P, 4, P]),
                                  bank[7][:, :].rearrange("p (u t) -> p u t", u=4))\
                    .then_inc(S("T_up"), 1)
                if s % 3 == 0:
                    weigh(s // 3)
                elif s % 3 == 1:
                    normalize(s // 3)
            dve.wait_ge(S("osum_mm"), 2)
            for t in range(2):
                i = ts(fsq[:, 2 * t:2 * t + 2, :], bank[(0, 5)[t]][:, :].rearrange("p (m t) -> p m t", m=2),
                       1.0 / HD, NORM_EPS, ALU.mult, ALU.add)
            i.then_inc(S("oms"), 1)
            dve.wait_ge(S("q_mm"), 1)
            tt(QT[:, :, :], bank[4][:, :].rearrange("p (m t) -> p m t", m=NF), R0[:, :, :], ALU.add)\
                .then_inc(S("QT_ready"), 1)
            dve.wait_ge(S("orms"), 1)
            step(v.reciprocal(fsq[:, :, :], fsq[:, :, :]))
            for t in range(2):
                i = tt(mix_f[:, 2 * t:2 * t + 2, :], bank[2 + t][:, :].rearrange("p (m t) -> p m t", m=2),
                       fsq[:, 2 * t:2 * t + 2, :], ALU.mult)
            step(i)
            dve.wait_ge(S("ogate"), 1)
            stt(mix_f[:, :, :], mix_f[:, :, :], colof('o_norm_g'), pf[:, 12:16, :], ALU.mult, ALU.mult)\
                .then_inc(S("mixf_ready"), 1)
            dve.wait_ge(S("ymean_mm"), 2)
            for t in range(2):
                i = stt(yT[:, 2 * t:2 * t + 2, :], bank[(4, 7)[t]][:, :].rearrange("p (m t) -> p m t", m=2), -1.0 / HD,
                        yT[:, 2 * t:2 * t + 2, :], ALU.mult, ALU.add)
            i.then_inc(S("yc_ready"), 1)
            dve.wait_ge(S("yvar_mm"), 2)
            for t in range(2):
                i = ts(yrs[:, 2 * t:2 * t + 2, :], bank[(0, 5)[t]][:, :].rearrange("p (m t) -> p m t", m=2),
                       1.0 / HD, GN_EPS, ALU.mult, ALU.add)
            i.then_inc(S("yms"), 1)
            dve.wait_ge(S("yrms"), 1)
            step(v.reciprocal(yrs[:, :, :], yrs[:, :, :]))
            step(tt(yT[:, :, :], yT[:, :, :], yrs[:, :, :], ALU.mult))
            for m in range(NF):
                i = ts(yT[:, m, :], yT[:, m, :], colof('gn_w', m), colof('gn_b', m), ALU.mult, ALU.add)
            step(i)
            step(tt(yT[:, :, :], yT[:, :, :], bonus[:, :, :], ALU.add))
            tt(mix_r[:, :, :], yT[:, :, :], g_f[:, :, :], ALU.mult).then_inc(S("mixr_ready"), 1)
            dve.wait_ge(S("late_in"), 16 * 5)
            step(stt(scale2[:, :], scale2[:, :], 1.0, n2g[:, :], ALU.add, ALU.mult))
            for j in range(NOUT):
                for t in range(TT):
                    n = 2 * j + t
                    cols = slice(j * NC, (j + 1) * NC)
                    dve.wait_ge(S("wo_mm"), n + 1)
                    step(tt(evac[:, t, :], bank[(2, 3, 1, 6)[n]][:, :], gate1[:, cols], ALU.mult))
                    tt(x1[:, t, cols], x1[:, t, cols], evac[:, t, :], ALU.add).then_inc(S("x1_ready"), 1)
            dve.wait_ge(S("ss_ready"), 2 * TT)
            ts(ss2[:, :], ss2[:, :], 1.0 / D, NORM_EPS, ALU.mult, ALU.add).then_inc(S("ms_ready"), 1)
            dve.wait_ge(S("rms_ready"), 2)
            step(v.reciprocal(rs2[:, :], rs2[:, :]))
            for t in range(TT):
                step(stt(h2[:, t, :], x1[:, t, :], rs2[:, t:t + 1], scale2[:, :], ALU.mult, ALU.mult))
                tt(h2[:, t, :], h2[:, t, :], shift2[:, :], ALU.add).then_inc(S("h2_ready"), 1)
            for t in range(TT):
                dve.wait_ge(S("h2_ready"), t + 1)
                dve.wait_ge(S("hhi_ready"), t + 1)
                tt(h_lo[:, t, :], h2[:, t, :], h_hi[:, t, :].bitcast(F32), ALU.subtract).then_inc(S("hlo_ready"), 1)
            dve.wait_ge(S("bias_T"), 1)
            bT = bank[7][:, :].rearrange("p (s e) -> p s e", e=NE)
            for cc in range(4):
                tile0 = (0, 8, 4, 12)[cc]
                i = ts(biasT[:, :, cc, :].rearrange("p e s -> p s e"), bT[:, tile0:tile0 + 4, :], float(cc % 2),
                       None, ALU.add)
            i.then_inc(S("biasT_ready"), 1)
            dve.wait_ge(S("late2_in"), 16 * 4)
            dve.wait_ge(S("late_consts"), 2)
            dve.wait_ge(S("router_mm"), 1)
            step(tt(logits[:, :, :], bank[6][:, 0:TT * NE].rearrange("p (t e) -> p t e", t=TT),
                    brt[:, :].unsqueeze(1).to_broadcast([P, TT, NE]), ALU.add))
            for t in range(TT):
                i = v.max(top8[:, t, :], logits[:, t, :])
            step(i)
            for t in range(TT):
                i = v.max_index(idx8[:, t, :], top8[:, t, :], logits[:, t, :])
            step(i)
            v.tensor_copy(idxf[:, :, :], idx8[:, :, :])
            tt(texp[:, :, :], top8[:, :, 0:TOPK], top8[:, :, 0:1].to_broadcast([P, TT, TOPK]), ALU.subtract)\
                .then_inc(S("tdiff"), 1)
            dve.wait_ge(S("texp_ready"), 1)
            step(v.tensor_reduce(tsum[:, :], texp[:, :, :], AX.X, ALU.add))
            step(v.reciprocal(tsum[:, :], tsum[:, :]))
            step(tt(texp[:, :, :], texp[:, :, :], tsum[:, :].unsqueeze(2).to_broadcast([P, TT, TOPK]), ALU.mult))
            for t in range(TT):
                for k in range(TOPK):
                    i = ts(gk[:, t, k, :], iota_e[:, :], idxf[:, t, k:k + 1], texp[:, t, k:k + 1],
                           ALU.is_equal, ALU.mult)
            step(i)
            step(v.tensor_reduce(gates[:, :, :], gk[:, :, :, :].rearrange("p t k e -> p t e k"), AX.X, ALU.add))
            ts(sel[:, :, :], gates[:, :, :], 0.0, None, ALU.is_gt).then_inc(S("sel_ready"), 1)
            dve.wait_ge(S("rank_mm"), 1)
            step(v.tensor_copy(cnt[:, :], bank[2][:, 2 * NE:3 * NE]))
            for j in range(4):
                i = ts(ge[:, j, :], cnt[:, :], float(CAP * j), None, ALU.is_gt if j else ALU.is_ge)
            step(i)
            step(v.tensor_reduce(nblk[:, :], ge[:, :, :].rearrange("p j e -> p e j"), AX.X, ALU.add))
            step(v.tensor_tensor_scan(binc[:, :], ones[:, 0:NE], nblk[:, :], 0.0, ALU.mult, ALU.add))
            step(tt(bexc[:, :], binc[:, :], nblk[:, :], ALU.subtract))
            step(ts(bexc[:, :], bexc[:, :], float(CAP), None, ALU.mult))
            step(tt(pos[:, :, :], bank[2][:, 0:TT * NE].rearrange("p (t e) -> p t e", t=TT),
                    bexc[:, :].unsqueeze(1).to_broadcast([P, TT, NE]), ALU.add))
            step(stt(pos[:, :, :], pos[:, :, :], 1.0, sel[:, :, :], ALU.add, ALU.mult))
            step(ts(pos[:, :, :], pos[:, :, :], -1.0, None, ALU.add))
            step(tt(icmp[:, :, :], binc[0:1, :].unsqueeze(1).to_broadcast([1, NI + 2, NE]),
                    iota_i[:, :].unsqueeze(2).to_broadcast([1, NI + 2, NE]), ALU.is_le))
            step(v.tensor_reduce(isum[:, :], icmp[:, :, :], AX.X, ALU.add))
            ts(items[:, :], isum[:, :], float(NE - 1), None, ALU.min).then_inc(S("items_ready"), 1)
            ts(last_item[:, :], binc[0:1, :], -1.0, None, ALU.add).then_inc(S("items_ready"), 1)
            ts(n_items[:, :], binc[0:1, NE - 1:NE].to_broadcast([1, 2]), float(-NE), None, ALU.add).then_inc(S("items_ready"), 1)
            dve.wait_ge(S("items_ready"), 3)
            dve.wait_ge(S("biasT_ready"), 1)
            v.memset(ss2[:, :], 0.0).then_inc(S("moe_free"), 1)

            K = 10

            class Body:

                def __init__(self, i):
                    self.i, self.at = i, {}

                def step(self, name, ins):
                    self.at[name] = len(self.at) + 1
                    ins.then_inc(S("item_step"), 1)

                def wait(self, name):
                    dve.wait_ge(S("item_step"), self.i * K + self.at[name])

            def lo(i, cc, h):
                dve.wait_ge(S("hi_ready"), 2 * (EC * i + cc) + h + 1)
                part = slice(4 * h, 4 * h + 4)
                tt(w_lo[:, cc % 2, part, :], raw[:, item_slot(cc), part, :],
                   w_hi[:, cc % 2, part, :].bitcast(F32), ALU.subtract).then_inc(S("dve_lo"), 1)

            def select(i):
                e_i = dve.value_load(items[0:1, bass.ds(i, 1)], min_val=0, max_val=NE - 1)
                for t in range(TT):
                    ins = ts(onehot[:, t, :, :], slots[:, :, :], pos[:, t, bass.ds(e_i, 1)], None, ALU.is_equal)
                ins.then_inc(S("onehot_ready"), 1)

            def pick_bias(i, body):
                e = dve.value_load(items[0:1, bass.ds(i, 1)], min_val=0, max_val=NE - 1)
                body.step("bias", v.tensor_copy(bias_i[:, :, :].rearrange("p c s -> p (c s)"),
                                                biasT[:, bass.ds(e, 1), :, :].rearrange("p e c s -> p (e c s)")))

            def pick_tokens(i, body):
                dve.wait_ge(S("gatehot_ready"), i + 1)
                body.step("slots", ts(slots[:, :, :], slots[:, :, :], float(CAP), None, ALU.add))
                body.wait("slots")
                select(i + 1)

            def joined(cc):
                dst = (gated, ups)[cc % 2][:, cc // 2, :, :]
                return dst, bank[ACC[cc]][:, :].rearrange("p (s a c) -> p s a c", s=4, a=2)

            def join_a(i, cc, body):
                dst, b = joined(cc)
                dve.wait_ge(S("turned"), 4 * i + cc + 1)
                if cc == 0:
                    body.wait("bias")
                if not isinstance(i, int):
                    dve.wait_ge(S("aT_ready"), 2 * i - 1 + cc // 2)
                body.step(f"a{cc}", tt(dst, b[:, :, 0, :], bias_i[:, cc, :].unsqueeze(2).to_broadcast([P, 4, CAP]),
                                       ALU.add))

            def join_b(i, cc, body):
                dst, b = joined(cc)
                body.wait(f"a{cc}")
                tt(dst, b[:, :, 1, :], dst, ALU.add).then_inc(S("tr_ev"), 1)

            def gate_min(i, pair):
                dve.wait_ge(S("tr_ev"), 4 * i + 2 * pair + 1)
                ts(gated[:, pair, :, :], gated[:, pair, :, :], LIMIT, None, ALU.min).then_inc(S("gate_ready"), 1)

            def up_clip(i, pair, body):
                dve.wait_ge(S("tr_ev"), 4 * i + 2 * pair + 2)
                body.step(f"clip{pair}", ts(ups[:, pair, :, :], ups[:, pair, :, :], 1.0 - LIMIT, 1.0 + LIMIT,
                                            ALU.max, ALU.min))

            def gate_sig(i, pair, body):
                dve.wait_ge(S("sig_ready"), 2 * i + pair + 1)
                body.step(f"sig{pair}", tt(gated[:, pair, :, :], gated[:, pair, :, :], sig[:, pair, :, :], ALU.mult))

            def act(i, pair, body):
                body.wait(f"clip{pair}")
                body.wait(f"sig{pair}")
                tt(gated[:, pair, :, :], gated[:, pair, :, :], ups[:, pair, :, :], ALU.mult)\
                    .then_inc(S("act_ready"), 1)

            def act_lo(i, pair):
                dve.wait_ge(S("aThi_ready"), 2 * i + pair + 1)
                part = slice(4 * pair, 4 * pair + 4)
                tt(aT[:, part, 1, :], gated[:, pair, :, :], aT[:, part, 0, :].bitcast(F32), ALU.subtract)\
                    .then_inc(S("aT_ready"), 1)

            def take_xT(i):
                dve.wait_ge(S("xThi_ready"), i + 1)
                tt(xT[:, :, 1, :], bank[3][:, :].rearrange("p (k c) -> p k c", k=KT),
                   xT[:, :, 0, :].bitcast(F32), ALU.subtract).then_inc(S("xT_ready"), 1)

            def item(i):
                body = Body(i)
                lo(i, 0, 0)
                take_xT(i)
                lo(i, 0, 1)
                lo(i, 1, 0)
                pick_tokens(i, body)
                lo(i, 2, 0)
                pick_bias(i, body)
                lo(i, 2, 1)
                join_a(i, 0, body)
                lo(i, 3, 0)
                join_a(i, 1, body)
                join_b(i, 0, body)
                join_b(i, 1, body)
                lo(i, 3, 1)
                gate_min(i, 0)
                lo(i, 4, 0)
                up_clip(i, 0, body)
                gate_sig(i, 0, body)
                join_a(i, 2, body)
                act(i, 0, body)
                lo(i, 4, 1)
                act_lo(i, 0)
                join_b(i, 2, body)
                join_a(i, 3, body)
                gate_min(i, 1)
                join_b(i, 3, body)
                up_clip(i, 1, body)
                gate_sig(i, 1, body)
                act(i, 1, body)
                lo(i, 5, 0)
                act_lo(i, 1)
                assert len(body.at) == K

            select(0)
            n_it = dve.value_load(n_items[0:1, 0:1], min_val=0, max_val=NI - NE) + NE
            item(0)
            with dve.Fori(1, n_it) as i:
                item(i)

            dve.wait_ge(S("end_in"), 16 * 3)
            dve.wait_ge(S("scattered"), 2 * n_it)
            for t in range(TT):
                for half in range(NOUT):
                    cols = slice(half * NC, (half + 1) * NC)
                    i = tt(yo[:, t, cols], bank[4 + 2 * t + half][:, :], gate2[:, cols], ALU.mult)
                step(i)
                tt(yo[:, t, :], yo[:, t, :], x1e[:, t * D:(t + 1) * D], ALU.add).then_inc(S("xo_ready"), 1)
            dve.wait_ge(S("ss_ready"), 3 * TT)
            ts(ss3[:, :], ss3[:, :], 1.0 / D, NORM_EPS, ALU.mult, ALU.add).then_inc(S("ms_ready"), 1)
            dve.wait_ge(S("rms_ready"), 3)
            step(v.reciprocal(rs3[:, :], rs3[:, :]))
            for t in range(TT):
                stt(yo[:, t, :], yo[:, t, :], rs3[:, t:t + 1], fg, ALU.mult, ALU.mult).then_inc(S("out_ready"), 1)

        @block.tensor
        def _(pe):
            mm, tr = nc.tensor.matmul, nc.tensor.transpose
            pe.wait_ge(S("consts"), 1)
            pe.wait_ge(S("rows_in"), 16 * NROWDMA)
            tr(bank[5][:, 0:NROW], rowv[:, :], ident[0:NROW, 0:NROW]).then_inc(S("rowsT"), 1)
            for k in range(KT):
                for t in range(TT):
                    pe.wait_ge(S("xn_ready"), t + 1)
                    i = tr(bank[k // 2][:, (k % 2) * T + t * P:(k % 2) * T + (t + 1) * P],
                           x_sb[:, t, k * P:(k + 1) * P], ident[:, :])
                if k % 2:
                    i.then_inc(S("xnT"), 1)
            for j in range(4):
                pe.wait_ge(S("ada_used"), j + 1)
                for s in range(4):
                    i = mm(bank[4][:, 4 * j + s:4 * j + s + 1], acc[:, j % 2, s * P:(s + 1) * P], ones[:, 0:1],
                           start=True, stop=True)
                i.then_inc(S("acc_used"), 1)
            mm(bank[4][:, 16:17], ident[:, :], ones[:, 0:1], start=True, stop=True).then_inc(S("col_mm"), 1)

            def project(m):
                n = where[('in', m // 4)]
                pe.wait_ge(*loaded(n))
                if m >= 4:
                    pe.wait_ge(S("p_ev"), m - 3)
                else:
                    pe.wait_ge(S("hT_ready"), KT)
                w = P if m < INT - 1 else NH
                for k in range(KT):
                    i = mm(bank[m % 4][0:w, 0:T], raw[:, slot_of(n), k, (m % 4) * P:(m % 4) * P + w], hT[:, k, :],
                           start=(k == 0), stop=(k == KT - 1))
                i.then_inc(S("p_mm"), 1)

            def mod_row(j):
                pe.wait_ge(S("ada_used"), 5 + j)
                o = bank[4][0:NROWS, :]
                if j == 0:
                    pe.wait_ge(S("modc_ready"), 1)
                    pe.wait_ge(S("brows_in"), 16)
                    mm(o, ident[0:NROWS, 0:NROWS], brows[:, :], start=True, stop=False)
                i = mm(o, pick[:, NROWS - j:2 * NROWS - j], acc[:, j % 2, :], start=False, stop=j == NROWS - 1)
                i.then_inc(S("acc_used"), 1)

            def head_sums(src, banks, done, acc_=None):
                for t in range(2):
                    mm(bank[banks[t]][:, :], blk[:, :], src[:, 2 * t:2 * t + 2, :].rearrange("p m t -> p (m t)"),
                       start=True, stop=True).then_inc(S(done), 1)

            for m in range(15):
                project(m)
                if m in (3, 7, 11, 14):
                    mod_row(m // 4)
            pe.wait_ge(S("lora_act"), 1)
            pe.wait_ge(S("lora_in"), 16 * 3)
            for q in range(6):
                if q >= 3:
                    pe.wait_ge(S("lora_ev"), q - 2)
                for t in range(2):
                    m = 2 * (q % 2) + t
                    o = bank[5 + q % 3][:, t * T:(t + 1) * T]
                    cols = slice(m * P, (m + 1) * P)
                    if q < 2:
                        i = mm(o, lora_w[0:HD, cols], loraa[0:HD, 0, :], start=True, stop=True)
                    elif q < 4:
                        i = mm(o, lora_w[HD:P, cols], loraa[HD:P, 0, :], start=True, stop=True)
                    else:
                        i = mm(o, g2_sb[:, cols], loraa[:, 1, :], start=True, stop=True)
                i.then_inc(S("lora_mm"), 1)
            for m in range(15, 20):
                project(m)
            mod_row(4)
            pe.wait_ge(S("kksq_ready"), 1)
            pe.wait_ge(S("consts"), 2)
            pe.wait_ge(S("lora_ev"), 6)
            head_sums(dtmp, (5, 6), "kksum_mm")
            for m in range(20, 24):
                project(m)
            mod_row(5)
            pe.wait_ge(S("rkk_ready"), 1)
            pe.wait_ge(S("kknorm"), 2)
            head_sums(dtmp, (5, 6), "bon_mm")
            for m in range(24, 28):
                project(m)
            mod_row(6)
            for m in range(28, INT):
                project(m)
            mod_row(7)
            pe.wait_ge(S("shifted"), 3)
            pe.wait_ge(S("bon_ev"), 2)
            for t in range(TT):
                for m in range(NF):
                    i = tr(bank[5 + t][:, m * P:(m + 1) * P], v_f[:, m, t * P:(t + 1) * P], ident[:, :])
                i.then_inc(S("tm_T"), 1)
            pe.wait_ge(S("p_ev"), INT)
            for n, (src, b) in enumerate(((A0, 7), (Kb, 0), (nBb, 1))):
                pe.wait_ge(S("tm_src"), n + 1)
                for m in range(NF):
                    i = tr(bank[b][:, m * P:(m + 1) * P], src[:, m, :], ident[:, :])
                i.then_inc(S("tm_T"), 1)
            pe.wait_ge(S("fsq_ready"), 1)
            head_sums(fsq, (2, 3), "fsum_mm")
            pe.wait_ge(S("fsq_ready"), 2)
            head_sums(fsq, (2, 3), "fsum_mm")
            pe.wait_ge(S("tm_ev"), 5)
            for t in range(TT):
                for m in range(NF):
                    i = tr(bank[5 + t][:, m * P:(m + 1) * P], pf[:, 8 + m, t * P:(t + 1) * P], ident[:, :])
                i.then_inc(S("fv_T"), 1)
            for u in range(NU):
                cc, (m, rows) = u // NH, tile_of(u % NH)
                b = bank[4 + u % 4]
                if u >= 4:
                    pe.wait_ge(S("lr_ev"), u - 3)
                elif u == 1:
                    pe.wait_ge(S("fv_ev"), 1)
                elif u == 2:
                    pe.wait_ge(S("fv_ev"), 2)
                ar = AR[rows, m, cc, :, :].rearrange("p b t -> p (b t)")
                mm(b[:, 0:2 * P], nBr[rows, m, cc, :], ar, start=True, stop=True)
                mm(b[:, 2 * P:4 * P], Kr[rows, m, cc, :], ar, start=True, stop=True).then_inc(S("lr_mm"), 1)
            pe.wait_ge(S("lr_ev"), NU)
            for u in range(NU):
                cc, h = u // NH, u % NH
                i = mm(bank[cc][:, h * HD:(h + 1) * HD], LR[:, u, 2, :], Vt[:, cc, h * HD:(h + 1) * HD],
                       start=True, stop=True)
                if h == NH - 1:
                    i.then_inc(S("mv_mm"), 1)
            pe.wait_ge(S("qk_ready"), 2)
            for g in (2, 3, 0, 1):
                if g == 0:
                    pe.wait_ge(S("mv_ev"), TT)
                for n in range(4):
                    i = tr(bank[g][:, n * P:(n + 1) * P], LR[:, 4 * g + n, 0, :], ident[:, :])
                i.then_inc(S("nL_T"), 1)
            pe.wait_ge(S("ncum_ready"), 1)

            def scores(h):
                m, rows = tile_of(h)
                if h:
                    pe.wait_ge(S("s_ev"), h)
                for t in range(TT):
                    n = (t + 1) * P
                    o = bank[0][:, t * P:t * P + n]
                    mm(o, pf[rows, m, t * P:(t + 1) * P], pf[rows, 4 + m, 0:n], start=True, stop=False)
                    i = mm(o, ident[0:NH, h:h + 1].to_broadcast([NH, P]), ncum[:, 0:n], start=False, stop=True)
                i.then_inc(S("s_mm"), 1)

            def turn_probs(h):
                pe.wait_ge(S("pr_ready"), h + 1)
                if h:
                    pe.wait_ge(S("prT_ready"), h)
                for b in range(3):
                    i = tr(bank[5][:, b * P:(b + 1) * P], pr[:, h % 2, b * P:(b + 1) * P], ident[:, :])
                i.then_inc(S("pr_T"), 1)

            def attend(h):
                m, rows = tile_of(h)
                pe.wait_ge(S("prT_ready"), h + 1)
                vcols = slice(h * HD, (h + 1) * HD)
                o = bank[2 + m // 2][rows, (m % 2) * T:(m % 2) * T + T]
                mm(o[:, 0:P], fvt[:, 0, vcols], prT[:, h % 2, 0:P], start=True, stop=True)
                mm(o[:, P:T], fvt[:, 0, vcols], prT[:, h % 2, P:2 * P], start=True, stop=False)
                mm(o[:, P:T], fvt[:, 1, vcols], prT[:, h % 2, 2 * P:3 * P], start=False, stop=True)\
                    .then_inc(S("o_mm"), 1)

            def level_x(s):
                g = s % 4
                pe.wait_ge(S("T_up"), s + 1 if s >= 4 else 4)
                if s >= 2:
                    pe.wait_ge(S("x_ev"), s - 1)
                for n in range(4):
                    u = 4 * g + n
                    i = mm(bank[(1, 4)[s % 2]][:, n * P:(n + 1) * P], LR[:, u, 0, :], Ti[:, u, :],
                           start=True, stop=True)
                i.then_inc(S("x_mm"), 1)

            def level_t(s):
                g, two = s % 4, s < STEPS - 4
                pe.wait_ge(S("x_ev"), s + 1)
                if s:
                    pe.wait_ge(S("T_up"), 4 + s)
                for n in range(4):
                    u = 4 * g + n
                    if two:
                        mm(bank[6][:, n * P:(n + 1) * P], TiT[:, u, :], XT_[:, s % 2, n, :], start=True, stop=True)
                    i = mm(bank[7][:, n * P:(n + 1) * P], XT_[:, s % 2, n, :], TiT[:, u, :], start=True, stop=True)
                i.then_inc(S("tt_mm"), 1)

            level_x(0)
            for s in range(STEPS):
                if s + 1 < STEPS:
                    level_x(s + 1)
                level_t(s)
                if s % 3 == 0:
                    if s:
                        attend(s // 3 - 1)
                    scores(s // 3)
                elif s % 3 == 2:
                    turn_probs(s // 3)
            attend(NH - 1)
            pe.wait_ge(S("T_up"), 4 + STEPS)
            for n, (cc, rhs, b) in enumerate(((0, MV[:, 0, :], 1), (1, MV[:, 1, :], 4), (1, A0t[:, :], 6))):
                for h in range(NH):
                    i = mm(bank[b][:, h * HD:(h + 1) * HD], TiT[:, cc * NH + h, :], rhs[:, h * HD:(h + 1) * HD],
                           start=True, stop=True)
                i.then_inc(S("tx_mm"), 1)
            pe.wait_ge(S("osq"), 2)
            head_sums(fsq, (0, 5), "osum_mm")

            def outputs(u, last_):
                cc, h = u // NH, u % NH
                m, rows = tile_of(h)
                vcols = slice(h * HD, (h + 1) * HD)
                o = bank[(1, 6)[m // 2]][rows, (m % 2) * T + cc * P:(m % 2) * T + (cc + 1) * P]
                mm(o, Vt[:, cc, vcols], LR[:, u, 3, :], start=True, stop=False)
                return mm(o, TMV[:, cc, vcols], LR[:, u, 1, :], start=False, stop=last_), o

            pe.wait_ge(S("tx_ev"), 1)
            for h in range(NH):
                m, rows = tile_of(h)
                vcols = slice(h * HD, (h + 1) * HD)
                o = bank[7][rows, m * HD:(m + 1) * HD]
                mm(o, Kbt[:, vcols], Vt[:, 0, vcols], start=True, stop=False)
                i = mm(o, nBbt[:, vcols], TMV[:, 0, vcols], start=False, stop=True)
            i.then_inc(S("z_mm"), 1)
            pe.wait_ge(S("tx_ev"), 3)
            for h in range(NH):
                m, rows = tile_of(h)
                i = mm(bank[4][rows, m * P:(m + 1) * P], TA[:, h * HD:(h + 1) * HD], LR[:, NH + h, 1, :],
                       start=True, stop=True)
            i.then_inc(S("q_mm"), 1)
            for u in range(NH):
                i, _ = outputs(u, True)
            i.then_inc(S("y_mm"), 1)
            pe.wait_ge(S("QT_ready"), 1)
            pe.wait_ge(S("z_ev"), 1)
            for u in range(NH, NU):
                m, rows = tile_of(u % NH)
                _, o = outputs(u, False)
                i = mm(o, Z1[rows, m, :], QT[rows, m, :], start=False, stop=True)
                if u % 4 == 3:
                    i.then_inc(S("y_mm"), 1)
            pe.wait_ge(S("yT_ready"), 2)
            head_sums(yT, (4, 7), "ymean_mm")
            pe.wait_ge(S("ysq_ready"), 1)
            pe.wait_ge(S("oms"), 1)
            head_sums(ysq, (0, 5), "yvar_mm")
            pe.wait_ge(S("mixf_ready"), 1)
            for j in range(NOUT):
                n = where[('out', j)]
                pe.wait_ge(*loaded(n))
                for t in range(TT):
                    o = bank[(2, 3, 1, 6)[2 * j + t]]
                    for n_k, k in enumerate((4, 5, 6, 7, 0, 1, 2, 3)):
                        if k == 0:
                            pe.wait_ge(S("mixr_ready"), 1)
                        src = mix_f[:, k - 4, t * P:(t + 1) * P] if k >= 4 else mix_r[:, k, t * P:(t + 1) * P]
                        i = mm(o[:, :], src, raw[:, slot_of(n), k, :], start=(n_k == 0), stop=(n_k == 7))
                    i.then_inc(S("wo_mm"), 1)
            pe.wait_ge(S("late2_in"), 16 * 4)
            pe.wait_ge(S("x1_ready"), 2)
            for s in range(16):
                i = tr(bank[7][:, s * NE:(s + 1) * NE], bgu[:, s * P:(s + 1) * P], ident[0:NE, 0:NE])
            i.then_inc(S("bias_T"), 1)
            pe.wait_ge(S("h2_ready"), TT)
            for n in range(4):
                for k in (2 * n, 2 * n + 1):
                    for t in range(TT):
                        i = tr(bank[2 + n][:, (k % 2) * T + t * P:(k % 2) * T + (t + 1) * P],
                               h2[:, t, k * P:(k + 1) * P], ident[:, :])
                i.then_inc(S("h2_T"), 1)
            pe.wait_ge(S("h2T_ready"), 4)
            for t in range(TT):
                for k in range(KT):
                    i = mm(bank[6][:, t * NE:(t + 1) * NE], h2T[:, k, t * P:(t + 1) * P], wr[:, k, :],
                           start=(k == 0), stop=(k == KT - 1))
            i.then_inc(S("router_mm"), 1)
            pe.wait_ge(S("sel_ready"), 1)
            pe.wait_ge(S("late_consts"), 2)
            mm(bank[2][:, 0:NE], stri[:, :], sel[:, 0, :], start=True, stop=True)
            mm(bank[2][:, NE:2 * NE], ones[:, :], sel[:, 0, :], start=True, stop=False)
            mm(bank[2][:, NE:2 * NE], stri[:, :], sel[:, 1, :], start=False, stop=True)
            mm(bank[2][:, 2 * NE:3 * NE], ones[:, :], sel[:, 0, :], start=True, stop=False)
            mm(bank[2][:, 2 * NE:3 * NE], ones[:, :], sel[:, 1, :], start=False, stop=True)\
                .then_inc(S("rank_mm"), 1)
            for t in range(TT):
                i = tr(bank[3][0:NE, t * P:(t + 1) * P], gates[:, t, :], ident[:, :])
            i.then_inc(S("gT_mm"), 1)
            pe.wait_ge(S("gT_ready"), 1)
            pe.wait_ge(S("biasT_ready"), 1)
            for t in range(TT):
                for half in range(NOUT):
                    i = mm(bank[4 + 2 * t + half][:, :], gT[:, t * P:(t + 1) * P], bdn[:, half * NC:(half + 1) * NC],
                           start=True, stop=False)
            i.then_inc(S("init_mm"), 1)

            def gather(i, half):
                pe.wait_ge(S("onehot_ready"), i + 1)
                if not isinstance(i, int):
                    pe.wait_ge(*((S("scat_ready"), i) if half == 0 else (S("xg_ready"), 2 * i + 1)))
                elif half == 0 and i:
                    pe.wait_ge(S("scat_ready"), i)
                elif half == 1:
                    pe.wait_ge(S("xg_ready"), 2 * i + 1)
                for n in range(2 * TT):
                    t, part = n // 2, (h_hi, h_lo)[n % 2]
                    g = mm(bank[3][:, :], onehot[:, t, :, :].rearrange("p a c -> p (a c)"),
                           part[:, t, half * NC:(half + 1) * NC], start=(n == 0), stop=(n == 2 * TT - 1))
                g.then_inc(S("xg_mm"), 1)

            def turn_tokens(i):
                pe.wait_ge(S("xg_ready"), 2 * i + 2)
                for k in range(KT):
                    g = mm(bank[3][:, k * CAP:(k + 1) * CAP], xg[0:CAP, k * P:(k + 1) * P],
                           ident[0:CAP, 0:CAP], is_transpose=k > 0, start=True, stop=True)
                g.then_inc(S("xT_mm"), 1)

            def turn_gates(i):
                pe.wait_ge(S("gatehot_ready"), i + 1)
                pe.wait_ge(S("xT_ready"), i + 1)
                for t in range(TT):
                    g = tr(bank[3][:, t * P:(t + 1) * P], gatehot[:, t, :, :].rearrange("p a c -> p (a c)"),
                           ident[:, :])
                g.then_inc(S("st_mm"), 1)

            def multiply(i, cc, h, quarters=(0, 1)):
                q = EC * i + cc
                looped = not isinstance(i, int)
                if h == 0 and 0 in quarters:
                    if cc == 0:
                        pe.wait_ge(S("xT_ready"), i + 1)
                        if looped:
                            pe.wait_ge(S("tr_ev"), 4 * i)
                    elif cc in (1, 2):
                        if looped:
                            pe.wait_ge(S("acc_ev"), EC * i - 2 + cc)
                    elif cc == 3:
                        pe.wait_ge(S("tr_ev"), 4 * i + 1)
                    elif cc == 4:
                        pe.wait_ge(S("tr_ev"), 4 * i + 3)
                        pe.wait_ge(S("aT_ready"), 2 * i + 1)
                    else:
                        pe.wait_ge(S("aT_ready"), 2 * i + 2)
                if 0 in quarters:
                    pe.wait_ge(*lo_done(i, cc, h))
                for j in range(4 * h + 2 * quarters[0], 4 * h + 2 * quarters[-1] + 2):
                    for w in (w_hi, w_lo):
                        if cc < 4:
                            o, src, k = bank[ACC[cc]], xT, j
                            start, stop = j == 0 and w is w_hi, j == KT - 1 and w is w_lo
                        else:
                            o, src, k = bank[ACC[4 + j % 2]], aT, 4 * (cc - 4) + j // 2
                            start, stop = k == 0 and w is w_hi, k == KT - 1 and w is w_lo
                        g = mm(o[:, :], src[:, k, :, :].rearrange("p a c -> p (a c)"), w[:, cc % 2, j, :],
                               start=start, stop=stop)
                if 1 in quarters:
                    g.then_inc(S("half_mm"), 1)

            def turn(i, cc):
                pe.wait_ge(S("acc_ev"), EC * i + cc + 1)
                for s in range(4):
                    g = tr(bank[ACC[cc]][:, s * P:(s + 1) * P], evac[:, cc % 3, s * P:(s + 1) * P], ident[:, :])
                g.then_inc(S("turned"), 1)

            def scatter(i, half, last_=False):
                pe.wait_ge(S("acc_ev"), EC * i + half + 5)
                pe.wait_ge(S("scat_ready"), i + 1)
                for t in range(TT):
                    g = mm(bank[4 + 2 * t + half][:, :], scat[:, t * P:(t + 1) * P], evac[:, (4 + half) % 3, :],
                           start=False, stop=last_)
                g.then_inc(S("scattered"), 1)

            def item(i, first):
                multiply(i, 0, 0, (0,))
                turn_gates(i)
                multiply(i, 0, 0, (1,))
                multiply(i, 0, 1)
                if not first:
                    scatter(i - 1, 0)
                multiply(i, 1, 0)
                multiply(i, 1, 1, (0,))
                turn(i, 0)
                multiply(i, 1, 1, (1,))
                multiply(i, 2, 0)
                turn(i, 1)
                multiply(i, 2, 1)
                if not first:
                    scatter(i - 1, 1)
                multiply(i, 3, 0)
                turn(i, 2)
                gather(i + 1, 0)
                multiply(i, 3, 1)
                gather(i + 1, 1)
                turn(i, 3)
                multiply(i, 4, 0)
                multiply(i, 4, 1, (0,))
                turn_tokens(i + 1)
                multiply(i, 4, 1, (1,))
                multiply(i, 5, 0)
                multiply(i, 5, 1)

            pe.wait_ge(S("items_ready"), 3)
            n_it = pe.value_load(n_items[0:1, 0:1], min_val=0, max_val=NI - NE) + NE
            pe.wait_ge(S("hlo_ready"), TT)
            gather(0, 0)
            gather(0, 1)
            turn_tokens(0)
            item(0, True)
            with pe.Fori(1, n_it) as i:
                item(i, False)
            scatter(n_it - 1, 0, True)
            scatter(n_it - 1, 1, True)


NROWDMA = 17


def kernel(**inputs):
    import numpy as np
    import concourse.bacc as bacc
    from concourse.bass_utils import run_bass_kernel_spmd

    nc = bacc.Bacc("TRN2", target_bir_lowering=False, num_devices=1)
    arrays, args = {}, []
    for name in _INS:
        a = np.ascontiguousarray(inputs[name])
        arrays[f"in_{name}"] = a
        args.append(nc.dram_tensor(f"in_{name}", a.shape, mybir.dt.from_np(a.dtype), kind="ExternalInput").ap())
    args.append(nc.dram_tensor("out", (1, T, D), F32, kind="ExternalOutput").ap())
    build(nc, *args)
    r = run_bass_kernel_spmd(nc, [arrays], core_ids=[0])
    return r.results[0]["out"]


_INS = ['x', 'c', 'w_ada', 'b_ada', 'norm1_g', 'w_in', 'mu_shift', 'w0', 'w2', 'a0', 'a2', 'g2', 'k_k', 'k_a',
        'r_k', 'gn_w', 'gn_b', 'b_f', 'q_norm_g', 'k_norm_g', 'o_norm_g', 'w_out', 'norm2_g', 'w_router',
        'b_router', 'w_gate_up', 'b_gate_up', 'w_down', 'b_down', 'final_g']
```
